# Optimizing a Trainium2 kernel written in Bass

```python
import math
import jax, jax.numpy as jnp
from jax import lax
import numpy as np

D_MODEL = 1024
BATCH = 1
SEQ = 256
DEPTH = 2

GRID_W = 64
CTX_LEN = 256
N_MIXERS = 3
D_FF = 2816
N_MOD = 9
EPS = 1e-6

SSD_D_INNER = 2 * D_MODEL
SSD_HEAD_DIM = 64
SSD_N_HEADS = SSD_D_INNER // SSD_HEAD_DIM
SSD_N_GROUPS = 4
SSD_D_STATE = 128
SSD_CONV_W = 5
SSD_CHUNK = 128
SSD_GN = SSD_N_GROUPS * SSD_D_STATE
SSD_CONV_DIM = SSD_D_INNER + 2 * SSD_GN
SSD_IN_DIM = SSD_D_INNER + SSD_CONV_DIM + 2 * SSD_N_HEADS

POOL_WINDOWS = (2, 4, 8, 16)
POOL_GROUPS = 4
POOL_GROUP_DIM = D_MODEL // POOL_GROUPS

HY_ORDER = 2
HY_SHORT_W = 3
HY_EMB_DIM = 33
HY_BANDS = (HY_EMB_DIM - 1) // 2
HY_FILTER_HIDDEN = 64
HY_MAX_DECAY = math.log(1e-2) / 0.3
HY_MIN_DECAY = math.log(1e-2) / 1.5


def rmsnorm(x, g):
    xf = x.astype(jnp.float32)
    y = xf * lax.rsqrt(jnp.mean(xf * xf, axis=-1, keepdims=True) + EPS)
    return (y * g.astype(jnp.float32)).astype(x.dtype)

def modulate(x, g, shift, scale):
    return rmsnorm(x, g) * (1 + scale) + shift

def swiglu(u, wg, wu, wd):
    return (jax.nn.silu(u @ wg) * (u @ wu)) @ wd

def dwconv_centred(u, w, b):
    K = w.shape[0]
    P = K // 2
    L = u.shape[1]
    up = jnp.pad(u, ((0, 0), (P, P), (0, 0)))
    out = b
    for k in range(K):
        out = out + w[k] * up[:, k:k + L]
    return out

def ssd_scan(x, dt, A, B, C, h0, with_output):
    b, l, H, P = x.shape
    G, N = B.shape[2], B.shape[3]
    E = H // G
    Q = SSD_CHUNK
    nc = l // Q
    xdt = (x.astype(jnp.float32) * dt[..., None]).reshape(b, nc, Q, G, E, P)
    Bc = B.astype(jnp.float32).reshape(b, nc, Q, G, N)
    Cc = C.astype(jnp.float32).reshape(b, nc, Q, G, N)
    a_cum = jnp.cumsum((dt * A).reshape(b, nc, Q, G, E), axis=2)
    a_last = a_cum[:, :, -1]
    decay_to_end = jnp.exp(a_last[:, :, None] - a_cum)
    states = jnp.einsum('bcsgn,bcsge,bcsgep->bcgepn', Bc, decay_to_end, xdt)

    def step(h, inp):
        st, al = inp
        return h * jnp.exp(al)[..., None, None] + st, h

    h_final, h_in = lax.scan(step, h0, (jnp.moveaxis(states, 1, 0), jnp.moveaxis(a_last, 1, 0)))
    if not with_output:
        return None, h_final
    h_in = jnp.moveaxis(h_in, 0, 1)
    seg = a_cum[:, :, :, None] - a_cum[:, :, None, :]
    mask = jnp.tril(jnp.ones((Q, Q), dtype=bool))[:, :, None, None]
    Lmat = jnp.exp(jnp.where(mask, seg, -jnp.inf))
    cb = jnp.einsum('bclgn,bcsgn->bclsg', Cc, Bc)
    y_diag = jnp.einsum('bclsg,bclsge,bcsgep->bclgep', cb, Lmat, xdt)
    y_off = jnp.einsum('bclgn,bcgepn,bclge->bclgep', Cc, h_in, jnp.exp(a_cum))
    y = (y_diag + y_off).reshape(b, l, H, P)
    return y.astype(x.dtype), h_final

def ssd_mixer(u_lat, u_ctx, w_in, conv_w, conv_b, a_log, dt_bias, d_skip, norm_g, w_out, need_ctx_out):
    H, P, G, N = SSD_N_HEADS, SSD_HEAD_DIM, SSD_N_GROUPS, SSD_D_STATE
    A = -jnp.exp(a_log.astype(jnp.float32))

    def project(u):
        b, l, _ = u.shape
        zxbcdt = u @ w_in
        z = zxbcdt[..., :SSD_D_INNER]
        xbc = jax.nn.silu(dwconv_centred(zxbcdt[..., SSD_D_INNER:SSD_D_INNER + SSD_CONV_DIM], conv_w, conv_b))
        dt_raw = zxbcdt[..., SSD_D_INNER + SSD_CONV_DIM:]
        xs = xbc[..., :SSD_D_INNER].reshape(b, l, H, P)
        Bm = xbc[..., SSD_D_INNER:SSD_D_INNER + SSD_GN].reshape(b, l, G, N)
        Cm = xbc[..., SSD_D_INNER + SSD_GN:].reshape(b, l, G, N)
        dt = jax.nn.softplus(dt_raw.reshape(b, l, 2, H).astype(jnp.float32) + dt_bias.astype(jnp.float32))
        return z, xs, Bm, Cm, dt

    def flip(t, d):
        return t[:, ::-1] if d == 1 else t

    zc, xc, Bc, Cc, dtc = project(u_ctx)
    zl, xl, Bl, Cl, dtl = project(u_lat)
    b = u_lat.shape[0]
    h0 = jnp.zeros((b, G, H // G, P, N), jnp.float32)
    y_lat = d_skip[:, None] * xl
    y_ctx = d_skip[:, None] * xc if need_ctx_out else None
    for d in range(2):
        yc, hc = ssd_scan(flip(xc, d), flip(dtc[:, :, d], d), A[d], flip(Bc, d), flip(Cc, d), h0, need_ctx_out)
        yl, _ = ssd_scan(flip(xl, d), flip(dtl[:, :, d], d), A[d], flip(Bl, d), flip(Cl, d), hc, True)
        y_lat = y_lat + flip(yl, d)
        if need_ctx_out:
            y_ctx = y_ctx + flip(yc, d)

    def gate_norm_out(y, z):
        b_, l_ = y.shape[:2]
        gy = (y.reshape(b_, l_, SSD_D_INNER) * jax.nn.silu(z)).reshape(b_, l_, G, SSD_D_INNER // G)
        gy = rmsnorm(gy, norm_g.reshape(G, SSD_D_INNER // G))
        return gy.reshape(b_, l_, SSD_D_INNER) @ w_out

    out_lat = gate_norm_out(y_lat, zl)
    out_ctx = gate_norm_out(y_ctx, zc) if need_ctx_out else None
    return out_lat, out_ctx

def box_sum(v, w, axis):
    L = v.shape[axis]
    cs = jnp.cumsum(v, axis=axis)
    pad = [(0, 0)] * v.ndim
    pad[axis] = (1, 0)
    cs = jnp.pad(cs, pad)
    pos = jnp.arange(L)
    hi = jnp.minimum(pos + (w - w // 2), L)
    lo = jnp.maximum(pos - w // 2, 0)
    s = jnp.take(cs, hi, axis=axis) - jnp.take(cs, lo, axis=axis)
    return s, (hi - lo).astype(jnp.float32)

def pool_grid(v, w):
    b, l, C = v.shape
    rows = l // GRID_W
    v4 = v.astype(jnp.float32).reshape(b, rows, GRID_W, C)
    s, cnt_c = box_sum(v4, w, 2)
    s, cnt_r = box_sum(s, w, 1)
    mean = s / (cnt_r[:, None, None] * cnt_c[None, :, None])
    return mean.reshape(b, l, C).astype(v.dtype) - v

def pool_seq(v, w):
    s, cnt = box_sum(v.astype(jnp.float32), w, 1)
    return (s / cnt[None, :, None]).astype(v.dtype) - v

def pool_mixer(u_lat, u_ctx, w, bias, scale, need_ctx_out):
    def mix(u, pool_fn):
        b, l, _ = u.shape
        grp = u.reshape(b, l, POOL_GROUPS, POOL_GROUP_DIM)
        pooled = jnp.stack([pool_fn(grp[:, :, g], POOL_WINDOWS[g]) for g in range(POOL_GROUPS)], axis=2)
        y = jnp.einsum('blgc,gcd->blgd', pooled, w) + bias
        return y.reshape(b, l, D_MODEL) * scale

    out_lat = mix(u_lat, pool_grid)
    out_ctx = mix(u_ctx, pool_seq) if need_ctx_out else None
    return out_lat, out_ctx

def hyena_filter_fft(L, fw1, fb1, fw2, fb2, fw3, ffreq):
    f32 = jnp.float32
    pos = jnp.arange(L, dtype=f32)
    t = jnp.linspace(0.0, 1.0, L, dtype=f32)
    wpos = 2.0 * math.pi * pos / L
    f = jnp.linspace(1e-4, HY_BANDS - 1, HY_BANDS, dtype=f32)
    ang = wpos[:, None] * f[None, :]
    z = jnp.concatenate([t[:, None], jnp.cos(ang), -jnp.sin(ang)], axis=-1)
    h = jnp.sin(ffreq[0].astype(f32) * (z @ fw1.astype(f32) + fb1.astype(f32)))
    h = jnp.sin(ffreq[1].astype(f32) * (h @ fw2.astype(f32) + fb2.astype(f32)))
    h = (h @ fw3.astype(f32)).reshape(L, HY_ORDER, 2, D_MODEL)
    deltas = jnp.abs(jnp.linspace(HY_MIN_DECAY, HY_MAX_DECAY, D_MODEL, dtype=f32))
    h = h * jnp.exp(-t[:, None, None, None] * deltas)
    h = h * lax.rsqrt(jnp.sum(h * h, axis=(0, 2), keepdims=True) + EPS)
    kern = jnp.concatenate([h[:, :, 0], jnp.zeros((1, HY_ORDER, D_MODEL), f32), h[:0:-1, :, 1]], axis=0)
    return jnp.fft.rfft(kern, axis=0)

def fftconv(u, kf, bias):
    L = u.shape[1]
    uf = u.astype(jnp.float32)
    y = jnp.fft.irfft(jnp.fft.rfft(uf, n=2 * L, axis=1) * kf, n=2 * L, axis=1)[:, :L]
    return (y + uf * bias.astype(jnp.float32)).astype(u.dtype)

def hyena_mixer(u_lat, u_ctx, w_in, conv_w, conv_b, fw1, fb1, fw2, fb2, fw3, ffreq, hbias, w_out, need_ctx_out):
    def run(u):
        kf = hyena_filter_fft(u.shape[1], fw1, fb1, fw2, fb2, fw3, ffreq)
        p = dwconv_centred(u @ w_in, conv_w, conv_b)
        v, x1, x2 = jnp.split(p, 3, axis=-1)
        z = x1 * fftconv(v, kf[:, 0], hbias[0])
        y = x2 * fftconv(z, kf[:, 1], hbias[1])
        return y @ w_out

    out_lat = run(u_lat)
    out_ctx = run(u_ctx) if need_ctx_out else None
    return out_lat, out_ctx

def n_layers_of(kind):
    return len(range(kind, DEPTH, N_MIXERS))

def first_inputs(seed: int = 0) -> dict:
    key = jax.random.key(seed)
    ks = jax.random.split(key, 32)
    f32 = jnp.float32

    def nrm(k, shape, scale):
        return jax.random.normal(k, shape, f32) * scale

    nA, nB, nC = n_layers_of(0), n_layers_of(1), n_layers_of(2)
    D, F = D_MODEL, D_FF
    H = SSD_N_HEADS
    dt0 = jnp.exp(jax.random.uniform(ks[12], (nA, 2, H), f32, math.log(1e-3), math.log(1e-1)))
    return {
        "x": nrm(ks[0], (BATCH, SEQ, D), 1.0),
        "c": nrm(ks[1], (BATCH, D), 1.0),
        "ctx": nrm(ks[2], (BATCH, CTX_LEN, D), 1.0),
        "c_ctx": nrm(ks[3], (D,), 1.0),
        "ada_w": nrm(ks[4], (DEPTH, D, N_MOD * D), 0.5 * D ** -0.5),
        "ada_b": nrm(ks[5], (DEPTH, N_MOD * D), 0.02),
        "norm_g": 1.0 + nrm(ks[6], (DEPTH, 3, D), 0.05),
        "ffn_w_gate": nrm(ks[7], (DEPTH, 2, D, F), D ** -0.5),
        "ffn_w_up": nrm(ks[8], (DEPTH, 2, D, F), D ** -0.5),
        "ffn_w_down": nrm(ks[9], (DEPTH, 2, F, D), F ** -0.5),
        "ssd_w_in": nrm(ks[10], (nA, D, SSD_IN_DIM), D ** -0.5),
        "ssd_conv_w": nrm(ks[11], (nA, SSD_CONV_W, SSD_CONV_DIM), SSD_CONV_W ** -0.5),
        "ssd_conv_b": nrm(ks[13], (nA, SSD_CONV_DIM), 0.02),
        "ssd_a_log": jnp.log(jax.random.uniform(ks[14], (nA, 2, H), f32, 1.0, 16.0)),
        "ssd_dt_bias": dt0 + jnp.log(-jnp.expm1(-dt0)),
        "ssd_d": 1.0 + nrm(ks[15], (nA, H), 0.1),
        "ssd_norm_g": 1.0 + nrm(ks[16], (nA, SSD_D_INNER), 0.05),
        "ssd_w_out": nrm(ks[17], (nA, SSD_D_INNER, D), SSD_D_INNER ** -0.5),
        "pool_w": nrm(ks[18], (nB, POOL_GROUPS, POOL_GROUP_DIM, POOL_GROUP_DIM), POOL_GROUP_DIM ** -0.5),
        "pool_b": nrm(ks[19], (nB, POOL_GROUPS, POOL_GROUP_DIM), 0.02),
        "pool_scale": 1.0 + nrm(ks[20], (nB, D), 0.1),
        "hy_w_in": nrm(ks[21], (nC, D, 3 * D), D ** -0.5),
        "hy_conv_w": nrm(ks[22], (nC, HY_SHORT_W, 3 * D), HY_SHORT_W ** -0.5),
        "hy_conv_b": nrm(ks[23], (nC, 3 * D), 0.02),
        "hy_filt_w1": nrm(ks[24], (nC, HY_EMB_DIM, HY_FILTER_HIDDEN), HY_EMB_DIM ** -0.5),
        "hy_filt_b1": nrm(ks[25], (nC, HY_FILTER_HIDDEN), 0.1),
        "hy_filt_w2": nrm(ks[26], (nC, HY_FILTER_HIDDEN, HY_FILTER_HIDDEN), HY_FILTER_HIDDEN ** -0.5),
        "hy_filt_b2": nrm(ks[27], (nC, HY_FILTER_HIDDEN), 0.1),
        "hy_filt_w3": nrm(ks[28], (nC, HY_FILTER_HIDDEN, HY_ORDER * 2 * D), HY_FILTER_HIDDEN ** -0.5),
        "hy_filt_freq": 1.0 + nrm(ks[29], (nC, 2, HY_FILTER_HIDDEN), 0.1),
        "hy_bias": nrm(ks[30], (nC, HY_ORDER, D), 0.1),
        "hy_w_out": nrm(ks[31], (nC, D, D), D ** -0.5),
        "final_g": 1.0 + nrm(jax.random.fold_in(key, 99), (D,), 0.05),
    }

def first_block(x, c, ctx, c_ctx, ada_w, ada_b, norm_g, ffn_w_gate, ffn_w_up, ffn_w_down,
              ssd_w_in, ssd_conv_w, ssd_conv_b, ssd_a_log, ssd_dt_bias, ssd_d, ssd_norm_g, ssd_w_out,
              pool_w, pool_b, pool_scale,
              hy_w_in, hy_conv_w, hy_conv_b, hy_filt_w1, hy_filt_b1, hy_filt_w2, hy_filt_b2, hy_filt_w3,
              hy_filt_freq, hy_bias, hy_w_out, final_g):
    h = ctx
    sc = jax.nn.silu(c)
    scc = jax.nn.silu(c_ctx)
    for i in range(DEPTH):
        kind = i % N_MIXERS
        j = i // N_MIXERS
        last = i == DEPTH - 1
        ctx_in_needed = (not last) or kind == 0
        m = (sc @ ada_w[i] + ada_b[i]).reshape(-1, N_MOD, D_MODEL)[:, :, None, :]
        mc = (scc @ ada_w[i] + ada_b[i]).reshape(N_MOD, D_MODEL)[:, None, None, :]

        x = x + 0.5 * m[:, 2] * swiglu(modulate(x, norm_g[i, 0], m[:, 0], m[:, 1]),
                                       ffn_w_gate[i, 0], ffn_w_up[i, 0], ffn_w_down[i, 0])
        if ctx_in_needed:
            h = h + 0.5 * mc[2] * swiglu(modulate(h, norm_g[i, 0], mc[0], mc[1]),
                                         ffn_w_gate[i, 0], ffn_w_up[i, 0], ffn_w_down[i, 0])

        u = modulate(x, norm_g[i, 1], m[:, 3], m[:, 4])
        uc = modulate(h, norm_g[i, 1], mc[3], mc[4]) if ctx_in_needed else None
        if kind == 0:
            y, yc = ssd_mixer(u, uc, ssd_w_in[j], ssd_conv_w[j], ssd_conv_b[j], ssd_a_log[j], ssd_dt_bias[j],
                              ssd_d[j], ssd_norm_g[j], ssd_w_out[j], not last)
        elif kind == 1:
            y, yc = pool_mixer(u, uc, pool_w[j], pool_b[j], pool_scale[j], not last)
        else:
            y, yc = hyena_mixer(u, uc, hy_w_in[j], hy_conv_w[j], hy_conv_b[j], hy_filt_w1[j], hy_filt_b1[j],
                                hy_filt_w2[j], hy_filt_b2[j], hy_filt_w3[j], hy_filt_freq[j], hy_bias[j],
                                hy_w_out[j], not last)
        x = x + m[:, 5] * y
        if not last:
            h = h + mc[5] * yc

        x = x + 0.5 * m[:, 8] * swiglu(modulate(x, norm_g[i, 2], m[:, 6], m[:, 7]),
                                       ffn_w_gate[i, 1], ffn_w_up[i, 1], ffn_w_down[i, 1])
        if not last:
            h = h + 0.5 * mc[8] * swiglu(modulate(h, norm_g[i, 2], mc[6], mc[7]),
                                         ffn_w_gate[i, 1], ffn_w_up[i, 1], ffn_w_down[i, 1])
    return rmsnorm(x, final_g)


MIX_WIDTH = 2 * D_MODEL
HEAD_DIM = 128
HGRN_WIDTH = MIX_WIDTH // 2
NSA_WIDTH = MIX_WIDTH - HGRN_WIDTH
HGRN_HEADS = HGRN_WIDTH // HEAD_DIM
NSA_HEADS = NSA_WIDTH // HEAD_DIM
NSA_KV_GROUPS = 2
NSA_HEADS_PER_GROUP = NSA_HEADS // NSA_KV_GROUPS
KV_WIDTH = NSA_KV_GROUPS * HEAD_DIM
N_BRANCHES = 3
HGRN_CHUNK = 64
CMP_BLOCK = 32
CMP_STRIDE = 16
SEL_BLOCK = 64
N_SELECT = 16
WINDOW = 512
Q_BLOCK = 128
ROPE_THETA = 500000.0
ROT_DIM = HEAD_DIM // 4
NORM_EPS = 1e-6
FORCE_SCORE = 1e4
IN_SPLITS = (HGRN_WIDTH, HGRN_WIDTH, HGRN_WIDTH, HGRN_WIDTH,
             NSA_WIDTH, KV_WIDTH, KV_WIDTH, KV_WIDTH, KV_WIDTH, KV_WIDTH, KV_WIDTH,
             NSA_HEADS * N_BRANCHES, NSA_WIDTH)
IN_COLS = sum(IN_SPLITS)


def rmsnorm_2(x, g):
    xf = x.astype(jnp.float32)
    y = xf * lax.rsqrt(jnp.mean(xf * xf, axis=-1, keepdims=True) + NORM_EPS)
    return (y * g.astype(jnp.float32)).astype(x.dtype)

def partial_rope(x, pos):
    half = ROT_DIM // 2
    inv = ROPE_THETA ** (-2.0 * jnp.arange(half, dtype=jnp.float32) / ROT_DIM)
    ang = pos.astype(jnp.float32)[:, None] * inv[None, :]
    cos = jnp.cos(ang)[None, :, None, :]
    sin = jnp.sin(ang)[None, :, None, :]
    xf = x.astype(jnp.float32)
    x1 = xf[..., :half]
    x2 = xf[..., half:ROT_DIM]
    out = jnp.concatenate([x1 * cos - x2 * sin, x2 * cos + x1 * sin, xf[..., ROT_DIM:]], axis=-1)
    return out.astype(x.dtype)

def masked_softmax(s, mask, axis):
    s = jnp.where(mask, s, -jnp.inf)
    m = jnp.max(s, axis=axis, keepdims=True)
    m = jnp.where(jnp.isfinite(m), m, 0.0)
    p = jnp.exp(s - m)
    return p / jnp.maximum(jnp.sum(p, axis=axis, keepdims=True), 1e-30)

def hgrn2_mixer(q, f_logit, i, lb):
    B, S, H, D = q.shape
    C = HGRN_CHUNK
    N = S // C
    log_f = jnp.logaddexp(jnp.log(lb), jnp.log1p(-lb) + jax.nn.log_sigmoid(f_logit.astype(jnp.float32)))
    k = -jnp.expm1(log_f)

    def chunks(a):
        return a.astype(jnp.float32).reshape(B, N, C, H, D).transpose(1, 0, 3, 2, 4)

    qc, kc, vc = chunks(q), chunks(k), chunks(i)
    bc = jnp.cumsum(chunks(log_f), axis=3)
    causal = jnp.tril(jnp.ones((C, C), dtype=bool))

    def step(state, xs):
        q_, k_, v_, b_ = xs
        o_inter = jnp.einsum('bhtk,bhkv->bhtv', q_ * jnp.exp(b_), state)
        diff = jnp.where(causal[:, :, None], b_[:, :, :, None, :] - b_[:, :, None, :, :], -jnp.inf)
        attn = jnp.einsum('bhtk,bhsk,bhtsk->bhts', q_, k_, jnp.exp(diff))
        o_intra = jnp.einsum('bhts,bhsv->bhtv', attn, v_)
        b_last = b_[:, :, -1:, :]
        state = state * jnp.exp(b_last[:, :, 0, :, None]) + jnp.einsum(
            'bhsk,bhsv->bhkv', k_ * jnp.exp(b_last - b_), v_)
        return state, o_inter + o_intra

    s0 = jnp.zeros((B, H, D, D), jnp.float32)
    _, o = lax.scan(step, s0, (qc, kc, vc, bc))
    return o.transpose(1, 0, 3, 2, 4).reshape(B, S, H, D).astype(q.dtype)

def compress(kv, pos_emb, w1, b1, w2):
    B, S, G, D = kv.shape
    n_cmp = (S - CMP_BLOCK) // CMP_STRIDE + 1
    idx = jnp.arange(n_cmp)[:, None] * CMP_STRIDE + jnp.arange(CMP_BLOCK)[None, :]
    blocks = kv[:, idx] + pos_emb[None, None, :, None, :]
    flat = blocks.transpose(0, 1, 3, 2, 4).reshape(B, n_cmp, G, CMP_BLOCK * D)
    return jax.nn.silu(flat @ w1 + b1) @ w2

def nsa_mixer(q, kc, vc, ks, vs, kw, vw, gate_logits, cmp_k, cmp_v):
    B, S, H, D = q.shape
    G, HG = NSA_KV_GROUPS, NSA_HEADS_PER_GROUP
    pos = jnp.arange(S)
    q = partial_rope(q, pos)
    ks = partial_rope(ks, pos)
    kw = partial_rope(kw, pos)
    k_cmp = compress(kc, *cmp_k)
    v_cmp = compress(vc, *cmp_v).astype(jnp.float32)
    n_cmp = k_cmp.shape[1]
    cmp_start = jnp.arange(n_cmp) * CMP_STRIDE
    cmp_end = cmp_start + CMP_BLOCK - 1
    k_cmp = partial_rope(k_cmp, cmp_end).astype(jnp.float32)
    n_sel_blocks = S // SEL_BLOCK
    n_top = min(N_SELECT, n_sel_blocks)
    sel_start = jnp.arange(n_sel_blocks) * SEL_BLOCK
    overlap = ((cmp_start[:, None] < sel_start[None, :] + SEL_BLOCK)
               & (cmp_start[:, None] + CMP_BLOCK > sel_start[None, :])).astype(jnp.float32)
    ks_blocks = ks.reshape(B, n_sel_blocks, SEL_BLOCK, G, D).transpose(0, 3, 1, 2, 4)
    vs_blocks = vs.reshape(B, n_sel_blocks, SEL_BLOCK, G, D).transpose(0, 3, 1, 2, 4)
    kw_pad = jnp.pad(kw, ((0, 0), (WINDOW, 0), (0, 0), (0, 0)))
    vw_pad = jnp.pad(vw, ((0, 0), (WINDOW, 0), (0, 0), (0, 0)))
    gates = jax.nn.sigmoid(gate_logits.astype(jnp.float32)).reshape(B, S, G, HG, N_BRANCHES)
    scale = HEAD_DIM ** -0.5
    b_idx = jnp.arange(B)[:, None, None, None]
    g_idx = jnp.arange(G)[None, :, None, None]
    blk = jnp.arange(n_sel_blocks)

    def query_block(qb):
        q0 = qb * Q_BLOCK
        t = q0 + jnp.arange(Q_BLOCK)
        qblk = lax.dynamic_slice_in_dim(q, q0, Q_BLOCK, axis=1).reshape(
            B, Q_BLOCK, G, HG, D).astype(jnp.float32)
        s_c = jnp.einsum('btghd,bngd->bghtn', qblk, k_cmp) * scale
        p_c = masked_softmax(s_c, cmp_end[None, :] <= t[:, None], -1)
        o_c = jnp.einsum('bghtn,bngd->btghd', p_c, v_cmp)
        imp = jnp.einsum('bghtn,nj->bgtj', p_c, overlap)
        cur = t // SEL_BLOCK
        forced = (blk[None, :] == 0) | (blk[None, :] == cur[:, None]) | (blk[None, :] == cur[:, None] - 1)
        valid = blk[None, :] * SEL_BLOCK <= t[:, None]
        imp = jnp.where(forced, FORCE_SCORE, jnp.where(valid, imp, -1.0))
        _, top = lax.top_k(imp, n_top)
        k_s = ks_blocks[b_idx, g_idx, top].astype(jnp.float32)
        v_s = vs_blocks[b_idx, g_idx, top].astype(jnp.float32)
        key_pos = top[..., None] * SEL_BLOCK + jnp.arange(SEL_BLOCK)
        mask_s = (key_pos <= t[None, None, :, None, None])[:, :, None]
        s_s = jnp.einsum('btghd,bgtnld->bghtnl', qblk, k_s) * scale
        p_s = masked_softmax(s_s, mask_s, (-2, -1))
        o_s = jnp.einsum('bghtnl,bgtnld->btghd', p_s, v_s)
        k_w = lax.dynamic_slice_in_dim(kw_pad, q0, WINDOW + Q_BLOCK, axis=1).astype(jnp.float32)
        v_w = lax.dynamic_slice_in_dim(vw_pad, q0, WINDOW + Q_BLOCK, axis=1).astype(jnp.float32)
        kp = q0 - WINDOW + jnp.arange(WINDOW + Q_BLOCK)
        mask_w = (kp[None, :] >= 0) & (kp[None, :] <= t[:, None]) & (t[:, None] - kp[None, :] < WINDOW)
        s_w = jnp.einsum('btghd,bkgd->bghtk', qblk, k_w) * scale
        p_w = masked_softmax(s_w, mask_w, -1)
        o_w = jnp.einsum('bghtk,bkgd->btghd', p_w, v_w)
        g = lax.dynamic_slice_in_dim(gates, q0, Q_BLOCK, axis=1)
        o = g[..., 0:1] * o_c + g[..., 1:2] * o_s + g[..., 2:3] * o_w
        return o.reshape(B, Q_BLOCK, H, D)

    out = lax.map(query_block, jnp.arange(S // Q_BLOCK))
    return out.transpose(1, 0, 2, 3, 4).reshape(B, S, H, D).astype(q.dtype)

def second_inputs(seed: int = 0) -> dict:
    key = jax.random.key(seed)
    k = jax.random.split(key, 16)

    def nrm(kk, shape, scale):
        return jax.random.normal(kk, shape, jnp.float32) * scale

    L, D = CMP_BLOCK, HEAD_DIM
    return {
        "x": nrm(k[0], (BATCH, SEQ, D_MODEL), 1.0),
        "pre_norm": 1.0 + nrm(k[1], (DEPTH, D_MODEL), 0.02),
        "post_norm": 1.0 + nrm(k[2], (DEPTH, D_MODEL), 0.02),
        "w_in": nrm(k[3], (DEPTH, D_MODEL, IN_COLS), D_MODEL ** -0.5),
        "hgrn_lb_logits": nrm(k[4], (DEPTH, HGRN_WIDTH), 0.5),
        "hgrn_out_norm": 1.0 + nrm(k[5], (DEPTH, HEAD_DIM), 0.02),
        "cmp_pos_k": nrm(k[6], (DEPTH, L, D), 0.1),
        "cmp_w1_k": nrm(k[7], (DEPTH, L * D, D), (L * D) ** -0.5),
        "cmp_b1_k": nrm(k[8], (DEPTH, D), 0.01),
        "cmp_w2_k": nrm(k[9], (DEPTH, D, D), D ** -0.5),
        "cmp_pos_v": nrm(k[10], (DEPTH, L, D), 0.1),
        "cmp_w1_v": nrm(k[11], (DEPTH, L * D, D), (L * D) ** -0.5),
        "cmp_b1_v": nrm(k[12], (DEPTH, D), 0.01),
        "cmp_w2_v": nrm(k[13], (DEPTH, D, D), D ** -0.5),
        "w_out": nrm(k[14], (DEPTH, MIX_WIDTH, D_MODEL), MIX_WIDTH ** -0.5),
    }

def second_block(x, pre_norm, post_norm, w_in, hgrn_lb_logits, hgrn_out_norm,
              cmp_pos_k, cmp_w1_k, cmp_b1_k, cmp_w2_k,
              cmp_pos_v, cmp_w1_v, cmp_b1_v, cmp_w2_v, w_out):
    B, S, _ = x.shape
    lb_probs = jax.nn.softmax(hgrn_lb_logits.astype(jnp.float32), axis=0)
    lower_bounds = jnp.maximum(jnp.cumsum(lb_probs, axis=0) - lb_probs[0:1], 0.0)
    offsets = np.cumsum(IN_SPLITS)[:-1].tolist()

    def heads(a):
        return a.reshape(B, S, -1, HEAD_DIM)

    for layer in range(DEPTH):
        h = rmsnorm_2(x, pre_norm[layer])
        proj = h @ w_in[layer]
        (hq, hf, hi, hz, nq, kc, vc, ks, vs, kw, vw, ng, nz) = jnp.split(proj, offsets, axis=-1)
        o_h = hgrn2_mixer(heads(hq), heads(hf), heads(hi),
                          lower_bounds[layer].reshape(HGRN_HEADS, HEAD_DIM))
        o_h = rmsnorm_2(o_h, hgrn_out_norm[layer]).reshape(B, S, HGRN_WIDTH) * jax.nn.silu(hz)
        o_n = nsa_mixer(heads(nq), heads(kc), heads(vc), heads(ks), heads(vs), heads(kw), heads(vw), ng,
                        (cmp_pos_k[layer], cmp_w1_k[layer], cmp_b1_k[layer], cmp_w2_k[layer]),
                        (cmp_pos_v[layer], cmp_w1_v[layer], cmp_b1_v[layer], cmp_w2_v[layer]))
        o_n = o_n.reshape(B, S, NSA_WIDTH) * jax.nn.silu(nz)
        y = jnp.concatenate([o_h, o_n], axis=-1).astype(x.dtype) @ w_out[layer]
        x = x + rmsnorm_2(y, post_norm[layer]).astype(x.dtype)
    return x


def setup_inputs(seed=0):
    out = dict(first_inputs(seed))
    for name, value in second_inputs(seed + 1).items():
        if name != "x":
            out[name + "_2"] = value
    return out


def reference(
    x, c, ctx, c_ctx, ada_w, ada_b, norm_g, ffn_w_gate, ffn_w_up, ffn_w_down, ssd_w_in,
    ssd_conv_w, ssd_conv_b, ssd_a_log, ssd_dt_bias, ssd_d, ssd_norm_g, ssd_w_out, pool_w,
    pool_b, pool_scale, hy_w_in, hy_conv_w, hy_conv_b, hy_filt_w1, hy_filt_b1, hy_filt_w2,
    hy_filt_b2, hy_filt_w3, hy_filt_freq, hy_bias, hy_w_out, final_g, pre_norm_2, post_norm_2,
    w_in_2, hgrn_lb_logits_2, hgrn_out_norm_2, cmp_pos_k_2, cmp_w1_k_2, cmp_b1_k_2, cmp_w2_k_2,
    cmp_pos_v_2, cmp_w1_v_2, cmp_b1_v_2, cmp_w2_v_2, w_out_2,
):
    x = first_block(
        x, c, ctx, c_ctx, ada_w, ada_b, norm_g, ffn_w_gate, ffn_w_up, ffn_w_down, ssd_w_in,
        ssd_conv_w, ssd_conv_b, ssd_a_log, ssd_dt_bias, ssd_d, ssd_norm_g, ssd_w_out, pool_w,
        pool_b, pool_scale, hy_w_in, hy_conv_w, hy_conv_b, hy_filt_w1, hy_filt_b1, hy_filt_w2,
        hy_filt_b2, hy_filt_w3, hy_filt_freq, hy_bias, hy_w_out, final_g,
    )
    return second_block(
        x, pre_norm_2, post_norm_2, w_in_2, hgrn_lb_logits_2, hgrn_out_norm_2, cmp_pos_k_2,
        cmp_w1_k_2, cmp_b1_k_2, cmp_w2_k_2, cmp_pos_v_2, cmp_w1_v_2, cmp_b1_v_2, cmp_w2_v_2,
        w_out_2,
    )


_drawn_inputs = setup_inputs


def setup_inputs(seed=0):
    import zlib

    import numpy as np

    out = dict(_drawn_inputs(seed))
    spreads = {}
    factors = {'pool_b': 3.416, 'cmp_pos_k_2': 8.0, 'cmp_b1_k_2': 64.0, 'cmp_b1_v_2': 8.0}
    for name, (base, spread) in spreads.items():
        noise = np.random.default_rng([zlib.crc32(name.encode()), seed]).standard_normal(out[name].shape)
        drawn = base * np.exp(spread * noise) if base else spread * noise
        out[name] = __import__('jax').numpy.asarray(drawn.astype(out[name].dtype))
    for name, factor in factors.items():
        out[name] = (out[name] * factor).astype(out[name].dtype)
    return out
```

```python
from contextlib import ExitStack

import numpy as np

import concourse.bass as bass
from concourse import mybir

F32 = mybir.dt.float32
F32R = mybir.dt.float32r
U8 = mybir.dt.uint8
ALU = mybir.AluOpType
ACT = mybir.ActivationFunctionType
AX = mybir.AxisListType

P = 128
T = 256
TT = T // P
D = 1024
KB = D // P
DEPTH = 2
N_MOD = 9
D_FF = 2816
FP = D_FF // 256
EPS = 1e-6
CH = 2048
SLOTS = 3

HEADS = 32
HP = 64
GROUPS = 4
EH = HEADS // GROUPS
INNER = HEADS * HP
NS = 128
CONV_DIM = INNER + 2 * GROUPS * NS
CONV_W = 5
PAD = CONV_W // 2
DT_COL = INNER + CONV_DIM - 64

WINDOWS = (2, 4, 8, 16)
GRID_W = 64

IN2 = 7704
H2 = 8
CMP_BLOCK, CMP_STRIDE = 32, 16
NCMP = (T - CMP_BLOCK) // CMP_STRIDE + 1
ROT = 32
THETA = 500000.0
SCALE = 128 ** -0.5
NEG = -1e30
LEVELS = (128, 64, 32, 16, 8, 4, 2, 1)

ADA_CHUNKS = N_MOD * D // 256
ADA_FIRST = 8
ADA_BOTH = 5 * D // 256
BOTH_PAIRS = (ADA_BOTH - ADA_FIRST) // 2
ADA_FFN = 2 * (FP - 1)
LAST_PAIRS = (DEPTH * ADA_CHUNKS - ADA_FIRST - 3 * ADA_FFN) // 2

STREAM = [("ffn0", 3 * FP), ("ffn1", 3 * FP), ("ssd_in", 21), ("ssd_out", 8), ("ffn2", 3 * FP), ("ffn3", 3 * FP),
          ("pool", 1), ("ffn4", 3 * FP), ("proj0", 31), ("cmp0", 4), ("out0", 8), ("proj1", 31), ("cmp1", 4),
          ("out1", 8)]
G = {}
_n = 0
for _name, _count in STREAM:
    G[_name] = _n
    _n += _count
CHUNKS = _n
CHUNK_FLOATS = {G["ssd_in"]: KB * P, G["proj0"] + 22: KB * 24, G["proj1"] + 22: KB * 24}
NORMS = ["ctx_f0", "lat_f0", "ctx_ssd", "lat_ssd", "lat_f1", "l1_f0", "l1_pool", "l1_f1", "final",
         "pre0", "post0", "pre1", "post1"]
N = {name: i for i, name in enumerate(NORMS)}
SPLIT_NORMS = [n for n in NORMS if n not in ("final", "post0", "post1")]
NSP = {name: i for i, name in enumerate(SPLIT_NORMS)}
SCALED = [n for n in NORMS if n != "final"]
NSC = {name: i for i, name in enumerate(SCALED)}
X_STAGES = ["load", "ffn0", "ffn1", "ssd_out", "ffn2", "ffn3", "pool", "ffn4", "final", "out0", "out1"]
XD = {name: 8 * (i + 1) for i, name in enumerate(X_STAGES)}

ROWS = {}
for _t, _items in enumerate([
    [("ada_b0", 128)],
    [("ada_b1", 16), ("norm_g", 48), ("conv_b", 24), ("final_g", 8), ("pre", 16), ("post", 16)],
    [("conv_w", 120), ("pool_b", 8)],
    [("pos_k", 64), ("pos_v", 64)],
    [("ssd_norm", 16), ("pool_scale", 8), ("c", 8), ("c_ctx", 8), ("lb", 16), ("out_norm", 2), ("b1_k", 2),
     ("b1_v", 2)],
]):
    _at = 0
    for _name, _rows in _items:
        ROWS[_name] = (_t, _at, _rows)
        _at += _rows
GATES_BY_POOL = (0, 1, 2)
UPS_BY_POOL = (0,)
DIAG_BANKS = ((0, 1), (3, 7))
G_BANKS = (0, 1, 2, 4)
ROW_TILES = 5
LAST_ROWS = 62


def shape_constants():
    ident = np.eye(P, dtype=np.float32)
    s, l = np.arange(P)[:, None], np.arange(P)[None, :]
    zero = np.zeros((P, P), np.float32)
    neg = lambda ok: np.where(ok, 0.0, NEG).astype(np.float32)
    mask_f = np.concatenate([neg(l >= s), zero], 1)
    mask_b = np.concatenate([zero, neg(l <= s)], 1)
    causal = neg(l <= s)
    t = np.arange(T)
    ends = np.arange(NCMP) * CMP_STRIDE + CMP_BLOCK - 1
    cmp_mask = np.full((TT, P, 16), NEG, np.float32)
    cmp_mask[:, :, :NCMP] = np.where(ends[None, :] <= t[:, None], 0.0, NEG).reshape(TT, P, NCMP)
    inv = np.float32(THETA) ** (np.float32(-2.0) * np.arange(ROT // 2, dtype=np.float32) / np.float32(ROT))

    def rope(pos):
        ang = pos.astype(np.float32)[None, :] * inv[:, None]
        return np.tile(np.cos(ang), (2, 1)).astype(np.float32), np.tile(np.sin(ang), (2, 1)).astype(np.float32)

    cos_t, sin_t = rope(t)
    cos_e, sin_e = rope(ends)
    rot = np.zeros((ROT, ROT), np.float32)
    half = ROT // 2
    for i in range(half):
        rot[half + i, i] = -1.0
        rot[i, half + i] = 1.0
    wide = np.zeros((P, 2 * T + 32 + ROT), np.float32)
    wide[:ROT, 0:T], wide[:ROT, T:2 * T] = cos_t, sin_t
    wide[:ROT, 2 * T:2 * T + NCMP], wide[:ROT, 2 * T + 16:2 * T + 16 + NCMP] = cos_e, sin_e
    wide[:ROT, 2 * T + 32:] = rot
    f32 = np.concatenate([ident, mask_f, mask_b, causal, cmp_mask[0], cmp_mask[1], wide], 1)
    levels = np.zeros((P, len(LEVELS), P), np.float32)
    for i, m in enumerate(LEVELS[1:]):
        levels[:, i] = (s // (2 * m) == l // (2 * m)) & (s % (2 * m) < m) & (l % (2 * m) >= m)
    levels[:, len(LEVELS) - 1] = s == l
    rows = T // GRID_W
    pool = np.zeros((len(WINDOWS), T, T), np.float32)
    for g, w in enumerate(WINDOWS):
        r_of, c_of = t // GRID_W, t % GRID_W
        for o in range(T):
            r, c = r_of[o], c_of[o]
            r0, r1 = max(r - w // 2, 0), min(r + w - w // 2, rows)
            c0, c1 = max(c - w // 2, 0), min(c + w - w // 2, GRID_W)
            inside = (r_of >= r0) & (r_of < r1) & (c_of >= c0) & (c_of < c1)
            pool[g, inside, o] = np.float32(1.0) / np.float32((r1 - r0) * (c1 - c0))
        pool[g] -= np.eye(T, dtype=np.float32)
    return f32, levels.reshape(P, -1), pool


def two_block_kernel(nc, a, out):
    ctx = ExitStack()
    with ctx:
        base = 16512
        KIB = 1024
        top = [base]

        def fixed(name, shape, dt=F32):
            nbytes = int(np.prod(shape[1:])) * (1 if dt == U8 else 4)
            t = nc.alloc_sbuf_tensor_at(name, shape, dt, offset=top[0])
            top[0] += (nbytes + 31) // 32 * 32
            return t

        raw = [fixed(f"raw{i}", [P, CH]) for i in range(SLOTS)]
        whi = [fixed(f"w_hi{i}", [P, CH], F32R) for i in range(SLOTS)]
        wlo = [fixed(f"w_lo{i}", [P, CH], F32R) for i in range(SLOTS)]
        x = fixed("x", [P, KB, T])
        u_at = top[0]
        u_hi = fixed("u_hi", [P, KB, T], F32R)
        u_lo = fixed("u_lo", [P, KB, T], F32R)
        scratch_at = top[0]
        scratch = fixed("scratch", [P, KB, T])
        NCONST = P + 2 * T + P + 32 + 2 * T + 32 + ROT
        consts = fixed("consts", [P, NCONST])
        ones = fixed("ones", [P, P])
        cols = fixed("cols", [P, ROW_TILES * P])
        mods_all = fixed("mods", [P, DEPTH * N_MOD * KB, 2])
        mods = [mods_all[:, l * N_MOD * KB:(l + 1) * N_MOD * KB, :] for l in range(DEPTH)]
        scv = fixed("silu_c", [P, KB, 2])
        mod_a = fixed("mod_scale", [P, KB])
        gate = fixed("gate", [P, KB])
        zero_col = fixed("zero_col", [P, 1])
        root_table = fixed("root_table", [P, 1])
        small = fixed("small", [P, 64])
        level_mask = fixed("level_mask", [P, len(LEVELS), P], U8)
        w2 = fixed("cmp_w2", [P, DEPTH, 2, P])
        region = top[0]
        room = 229344 - region

        def over(name, shape, off, dt=F32):
            assert off + int(np.prod(shape[1:])) * (1 if dt == U8 else 4) <= room, (name, off, room)
            return nc.alloc_sbuf_tensor_at(name, shape, dt, offset=region + off)

        ada = [over(f"ada{i}", [P, KB, 256], (0, 8, 72, 80, 16, 24)[i] * KIB) for i in range(ADA_FIRST - 2)]
        ada += [nc.alloc_sbuf_tensor_at(f"ada{6 + i}", [P, KB, 256], F32, offset=u_at + 8 * i * KIB) for i in range(2)]
        ada_acc = [over(f"ada_acc{i}", [P, 2, 256], (56 + 2 * i) * KIB) for i in range(2)]
        uc_hi = over("uc_hi", [P, KB, T], 16 * KIB, F32R)
        uc_lo = over("uc_lo", [P, KB, T], 24 * KIB, F32R)
        xc = over("x_ctx", [P, KB, T], 32 * KIB)
        hs = over("h_silu", [P, 512], 40 * KIB)
        hf = over("h_full", [P, 512], 42 * KIB)
        h_hi = over("h_hi", [P, 2, T], 44 * KIB, F32R)
        h_lo = over("h_lo", [P, 2, T], 46 * KIB, F32R)
        rms = [over(f"rms{i}", [P, T], (60 + i) * KIB) for i in range(2)]
        rstd = [over(f"rstd{i}", [P, T], (62 + i) * KIB) for i in range(2)]
        rows = over("rows", [P, ROW_TILES, P], 48 * KIB)
        x_in = [over(f"x_in{i}", [P, TT, D], 52 * KIB + 8 * KIB * i) for i in range(2)]
        mask_in = over("mask_in", [P, len(LEVELS), P], 68 * KIB)
        BT = over("B_T", [P, GROUPS, T], 0)
        CT = over("C_T", [P, GROUPS, T], 4 * KIB)
        Bc_tok = over("B_ctx_tok", [P, TT, GROUPS * NS], 8 * KIB)
        tokc = over("tok_cols", [P, 4, TT, 64], 12 * KIB)
        q_rows = over("q_rows", [P, T], 14 * KIB)
        dcol = over("d_skip", [P, HEADS], 15 * KIB)
        acol = over("a_cols", [P, 8], 15 * KIB + 128)
        sz = over("z_silu", [P, TT, INNER], 16 * KIB)
        dtt = [over(f"dt_tmp{i}", [P, 2 * T], 32 * KIB + 2 * KIB * i) for i in range(7)]
        hc = over("h_ctx", [P, 2, GROUPS, 512], 32 * KIB)
        xl_tok = over("x_tok", [P, TT, INNER], 48 * KIB)
        xw = [over(f"xw{i}", [P, 2, TT, 512], 64 * KIB + 8 * KIB * i) for i in range(2)]
        y = over("y", [P, TT, INNER], 64 * KIB)
        cpad = [over(f"conv_pad{i}", [P, 2, 2, T + 2 * PAD], 80 * KIB + 4224 * i) for i in range(2)]
        xsil = nc.alloc_sbuf_tensor_at("x_silu", [P, 2, 2, T], F32, offset=scratch_at)
        cacc = nc.alloc_sbuf_tensor_at("conv_acc", [P, 2, 2, T], F32, offset=scratch_at + 4 * KIB)
        qb = over("q_bcast", [P, EH, T], 32 * KIB)
        e_long = [over("e_long0", [P, EH, T], 40 * KIB),
                  nc.alloc_sbuf_tensor_at("e_long1", [P, EH, T], F32, offset=scratch_at)]
        e_short = [over(f"e_short{i}", [P, EH, P], 80 * KIB + 4 * KIB * i) for i in range(2)]
        cb = over("cb", [P, TT, T], 88 * KIB)
        q_first = [over(f"q_first{i}", [P, EH // 2, T], (8, 84)[i] * KIB) for i in range(2)]
        sq_dump = over("sq_dump", [P, TT, 512], 8 * KIB)
        tmp_off = nc.alloc_sbuf_tensor_at("y_off", [P, 2, 512], F32, offset=scratch_at)
        g_hi = over("g_hi", [P, INNER // P, T], 32 * KIB, F32R)
        g_lo = over("g_lo", [P, INNER // P, T], 16 * KIB, F32R)
        pool_m = over("pool_m", [P, 2 * len(WINDOWS), T], 48 * KIB)
        pq = over("pool_q", [P, TT, len(WINDOWS), T], 56 * KIB)
        ps_cols = over("pool_cols", [P, 2, KB], 64 * KIB)
        hq = over("hgrn_q", [P, H2, T], 0)
        hb = over("hgrn_b", [P, H2, T], 8 * KIB)
        hk = over("hgrn_k", [P, H2, T], 16 * KIB)
        hv = over("hgrn_v", [P, TT, D], 24 * KIB)
        szh = over("hgrn_gate", [P, H2, T], 32 * KIB)
        nq = over("nsa_q", [P, H2, T], 40 * KIB)
        snz = over("nsa_gate", [P, H2, T], 48 * KIB)
        kvc = over("kv_cmp", [P, 2, 2, T], 56 * KIB)
        ksw = over("k_sel_win", [P, 2, 2, T], 60 * KIB)
        vsw = over("v_sel_win", [P, 2, TT, 256], 64 * KIB)
        qk = over("qk", [P, H2, T], 68 * KIB)
        attn = over("attn", [P, H2, TT, P], 76 * KIB)
        attn_off = over("attn_off", [P, H2, P], 84 * KIB)
        gates = over("gates", [P, TT, 24], 88 * KIB)
        kcmp = over("k_cmp", [P, 2, 16], 88 * KIB + 256)
        vcmp = over("v_cmp", [P, 2, P], 88 * KIB + 512)
        hid = over("cmp_hidden", [P, 2, 16], 89 * KIB + 512)
        sums = over("soft_sums", [P, 64], 90 * KIB)
        o_h = over("o_hgrn", [P, H2, T], 16 * KIB)
        fin_hi = nc.alloc_sbuf_tensor_at("fin_hi", [P, 2 * KB, T], F32R, offset=u_at)
        fin_lo = over("fin_lo", [P, 2 * KB, T], 0, F32R)
        win = [over(f"cmp_in{i}", [P, CMP_BLOCK, 2, 16], (68, 8)[i] * KIB) for i in range(2)]
        win_hi = [over(f"cmp_in_hi{i}", [P, CMP_BLOCK, 2, 16], (72, 80)[i] * KIB, F32R) for i in range(2)]
        win_lo = [over(f"cmp_in_lo{i}", [P, CMP_BLOCK, 2, 16], (76, 84)[i] * KIB, F32R) for i in range(2)]
        pr1 = over("p_tile1", [P, H2, T], 24 * KIB)
        pr0 = over("p_tile0", [P, H2, P], 12 * KIB)
        pt0 = over("pt_keys0", [P, H2, T], 72 * KIB)
        pt1 = over("pt_keys1", [P, H2, P], 80 * KIB)
        ptc = over("pt_cmp", [P, H2, T], 16 * KIB)
        prc = over("p_cmp", [P, TT, H2, 16], 84 * KIB)
        y_out = over("y_out", [P, KB, T], 72 * KIB)
        x_out = over("x_out", [P, TT, D], 24 * KIB)

        ident = consts[:, 0:P]
        rtmp = consts[0:ROT, P:P + 2 * T].rearrange("p (g t) -> p g t", t=T)
        mask_f, mask_b = consts[:, P:P + T], consts[:, P + T:P + 2 * T]
        causal = consts[:, P + 2 * T:2 * P + 2 * T]
        _o = 2 * P + 2 * T
        cmp_mask = [consts[:, _o + 16 * i:_o + 16 * i + 16] for i in range(TT)]
        _o += 32
        cos_t, sin_t = consts[0:ROT, _o:_o + T], consts[0:ROT, _o + T:_o + 2 * T]
        _o += 2 * T
        cos_e, sin_e = consts[0:ROT, _o:_o + 16], consts[0:ROT, _o + 16:_o + 32]
        rot = consts[0:ROT, _o + 32:_o + 32 + ROT]

        def col(name):
            tile, at, n = ROWS[name]
            return cols[:, tile * P + at:tile * P + at + n]

        bank = [ctx.enter_context(nc.psum_tensor(f"bank{i}", [P, 512], F32)) for i in range(8)]

        sem = {}

        def make(*names):
            for name in names:
                sem[name] = ctx.enter_context(nc.semaphore(name))

        make("consts_in", "rows_in", "x_in", "mask_in", "w2_in", "ssd_in", "pool_in", "set_up")
        landed = [ctx.enter_context(nc.semaphore(f"chunk_in{i}")) for i in range(SLOTS)]
        lo_done = [ctx.enter_context(nc.semaphore(f"lo_done{i}")) for i in range(SLOTS)]
        ada_in = [ctx.enter_context(nc.semaphore(f"ada_in{i}")) for i in range(ADA_FIRST)]
        make("hi_done", "chunk_used",
             "ada_done", "ada_acc", "ada_step", "mods_done", "silu_c",
             "cols_turned", "cols_done", "x_turned", "x_done",
             "squares", "stat_done", "root_done", "recip_done", "scaled", "u_hi_done", "u_done",
             "silu_done", "mult_done", "h_hi_done", "h_done", "y_done",
             "dve_step", "act_step")
        make("dt_taken", "dt_exp", "dt_cols", "tok_turned", "tok_done", "q_stored", 
             "conv_in", "conv_done", "conv_silu", "turned", "lat_kept", "ctx_kept", "state_done", "state_kept",
             "skip_done", "off_done", "off_added", "cb_done", "cb_kept", "z_kept", "seg_done", "e_done", "m_done",
             "diag_done", "y_added", "gated", "g_root", "g_norm", "g_turned", "g_hi_kept", "g_ready")
        make("pool_first", "pool_kept", "pool_done", "pool_cols")
        make("proj_kept", "lev_diff", "lev_exp", "lev_ready", "lev_done", "lev_kept", "off_kept", "attn_zero", "lb_diff", "lb_exp",
             "hgrn_step_v", "hgrn_step_a", "scan_done", "av_done", "o_kept", "o_sq", "o_stat", "o_root", "o_recip", "o_rstd",
             "o_gated", "fin_hi_done", "fin_done", "roped", "rope_done", "win_made", "win_hi_done", "win_done", "cmp_done",
             "cmp_silu", "cmp_out", "cmp_kept", "cmp_rot", "cmp_ready", "c_score", "c_diff", "c_exp", "c_prob",
             "c_turned", "c_kept", "c_av", "score_done", "score_max", "score_exp", "prob_done", "p_turned",
             "p_kept_a", "p_kept_v", "av2_done", "n_gated", "out_kept", "x_out_turned", "x_out_kept", "stored")
        q_first_loaded = [ctx.enter_context(nc.semaphore(f"q_first_loaded{i}")) for i in range(2)]
        q_loaded = [ctx.enter_context(nc.semaphore(f"q_loaded{i}")) for i in range(2)]
        S = sem

        q_scratch = nc.dram_tensor("q_scratch", [2 * HEADS, T], F32, kind="Internal").ap()

        def kxn(w):
            return w.rearrange("(k p) n -> p k n", p=P)

        def chunk(c, k, n):
            return [b[c % SLOTS][:, 0:k * n].rearrange("p (k n) -> p k n", k=k) for b in (whi, wlo)]

        SSD_COLS = [INNER + 256 * c for c in (8, 9, 10, 11, 0, 1, 2, 3, 4, 5, 6, 7)]
        CONV_IN = [2, 4, 5, 6] + [6 + 2 * i for i in range(1, 9)]
        CONV_SILU = [2, 4, 5, 6] + [6 + i for i in range(1, 9)]
        FFNS = [("ffn0", 0, 0), ("ffn1", 0, 0), ("ffn2", 0, 1), ("ffn3", 1, 0), ("ffn4", 1, 1)]
        ADA_PAIRS = [((1, BOTH_PAIRS + 1, 2), (BOTH_PAIRS + 1, FP, 1)), ((1, FP, 1),), ((1, FP, 1),),
                     ((1, LAST_PAIRS + 1, 1), (LAST_PAIRS + 1, FP, 0)), ((1, FP, 0),)]
        PROJ = ([(1024 + 256 * i, 256, False) for i in range(4)] + [(256 * i, 256, False) for i in range(4)]
                + [(2048 + 256 * i, 256, True) for i in range(4)]
                + [(5120, 256, False), (5376, 256, False), (5632, 256, False), (6144, 256, False),
                   (5888, 256, True), (6400, 256, True)]
                + [(4096 + 256 * i, 256, False) for i in range(4)] + [(6656, 24, True)]
                + [(3072 + 256 * i, 256, False) for i in range(4)] + [(6680 + 256 * i, 256, False) for i in range(4)])
        NP_ = len(PROJ)
        TURNS = [(0, 0), (0, 1), (1, 0), (2, 0), (1, 1), (2, 1)]
        NL = len(LEVELS)
        LEVEL_AT = lambda i: 11 + 2 * i
        DIAG_AT, AV_AT = 9, 27
        ROPE_AT = [16, 17, 22, 23, 24, 25]

        def halves(t, half):
            return t[:, :, :].rearrange("p h (r two m) -> p (h r) two m", two=2, m=half)

        block = ctx.enter_context(nc.Block())
        row_src = {"ada_b0": a["ada_b"].rearrange("l (r p) -> (l r) p", p=P)[0:P],
                   "ada_b1": a["ada_b"].rearrange("l (r p) -> (l r) p", p=P)[P:P + 16],
                   "norm_g": a["norm_g"].rearrange("l n (k p) -> (l n k) p", p=P),
                   "conv_b": a["ssd_conv_b"].rearrange("o (k p) -> (o k) p", p=P),
                   "final_g": a["final_g"].rearrange("(k p) -> k p", p=P),
                   "pre": a["pre_norm_2"].rearrange("l (k p) -> (l k) p", p=P),
                   "post": a["post_norm_2"].rearrange("l (k p) -> (l k) p", p=P),
                   "conv_w": a["ssd_conv_w"].rearrange("o w (k p) -> (o w k) p", p=P),
                   "pool_b": a["pool_b"].rearrange("o g (k p) -> (o g k) p", p=P),
                   "pos_k": a["cmp_pos_k_2"].rearrange("l n p -> (l n) p"),
                   "pos_v": a["cmp_pos_v_2"].rearrange("l n p -> (l n) p"),
                   "ssd_norm": a["ssd_norm_g"].rearrange("o (k p) -> (o k) p", p=P),
                   "pool_scale": a["pool_scale"].rearrange("o (k p) -> (o k) p", p=P),
                   "c": a["c"].rearrange("o (k p) -> (o k) p", p=P),
                   "c_ctx": a["c_ctx"].rearrange("(k p) -> k p", p=P),
                   "lb": a["hgrn_lb_logits_2"].rearrange("l (k p) -> (l k) p", p=P),
                   "out_norm": a["hgrn_out_norm_2"], "b1_k": a["cmp_b1_k_2"], "b1_v": a["cmp_b1_v_2"]}

        @block.sync
        def _(sp):
            def load(c, src, n, j=0):
                slot = c % SLOTS
                if c >= SLOTS:
                    sp.wait_ge(lo_done[slot], c // SLOTS + j)
                dst = raw[slot][:, 0:n]
                if len(src.shape) == 3:
                    dst = dst.rearrange("p (k n) -> p k n", k=src.shape[1])
                sp.dma_start(dst, src).then_inc(landed[slot], 16)

            def ffn(i):
                name, l, s = FFNS[i]
                g = G[name]
                wg, wu = kxn(a["ffn_w_gate"][l, s]), kxn(a["ffn_w_up"][l, s])
                wd = kxn(a["ffn_w_down"][l, s])
                def cols256(w, j):
                    return w[:, :, bass.ds(256 * j, 256)]

                load(g, cols256(wg, 0), CH)
                load(g + 1, cols256(wu, 0), CH)
                load(g + 2, cols256(wg, 1), CH)

                def pair(j, more):
                    load(g + 3, wd[:, bass.ds(2 * j - 2, 2), :], CH, j - 1)
                    load(g + 4, cols256(wu, j), CH, j - 1)
                    if more:
                        load(g + 5, cols256(wg, j + 1), CH, j - 1)

                with sp.Fori(1, FP - 1) as j:
                    pair(j, True)
                pair(FP - 1, False)
                load(g + 3 * FP - 1, wd[:, 2 * FP - 2:2 * FP, :], CH)

            for name, (t, at, n) in ROWS.items():
                sp.dma_start(rows[at:at + n, t, :], row_src[name]).then_inc(S["rows_in"], 16)
            sp.wait_ge(ada_in[5], 16)
            ffn(0)
            ffn(1)
            g = G["ssd_in"]
            w = kxn(a["ssd_w_in"][0])
            load(g, w[:, :, DT_COL:DT_COL + P], KB * P)
            for i, c0 in enumerate(SSD_COLS + [256 * z for z in range(8)]):
                load(g + 1 + i, w[:, :, c0:c0 + 256], CH)
            g = G["ssd_out"]
            w = kxn(a["ssd_w_out"][0])
            for o in range(4):
                for kh in range(2):
                    c = g + 2 * o + kh
                    load(c, w[:, 8 * kh:8 * kh + 8, 256 * o:256 * o + 256], CH)
            ffn(2)
            ffn(3)
            c = G["pool"]
            load(c, a["pool_w"][0].rearrange("g (k p) d -> p (g k) d", p=P), CH)
            ffn(4)
            for l in range(DEPTH):
                w = kxn(a["w_in_2"][l])
                g = G[f"proj{l}"]
                for i, (c0, n, _tok) in enumerate(PROJ):
                    load(g + i, w[:, :, c0:c0 + n], KB * n)
                g = G[f"cmp{l}"]
                for i in range(4):
                    w = a["cmp_w1_k_2" if i < 2 else "cmp_w1_v_2"][l].rearrange("(l p) n -> p l n", p=P)
                    load(g + i, w[:, 16 * (i % 2):16 * (i % 2) + 16, :], CH)
                g = G[f"out{l}"]
                w = kxn(a["w_out_2"][l])
                for o in range(4):
                    for kh in range(2):
                        c = g + 2 * o + kh
                        load(c, w[:, 8 * kh:8 * kh + 8, 256 * o:256 * o + 256], CH)
            sp.wait_ge(S["x_out_kept"], 4)
            for t in range(TT):
                sp.dma_start(out[0, t * P:(t + 1) * P, :], x_out[:, t, :]).then_inc(S["stored"], 16)
            sp.wait_ge(S["stored"], 16 * TT)

        @block.gpsimd
        def _(pool):
            def load_ada(q, slot, layer):
                src = kxn(a["ada_w"][layer])[:, :, bass.ds((q - layer * ADA_CHUNKS) * 256, 256)]
                pool.dma_start(ada[slot][:, :, :], src).then_inc(ada_in[slot], 16)

            pool.memset(cols[:, :], 0.0).then_inc(S["set_up"], 1)
            pool.memset(ones[:, :], 1.0).then_inc(S["set_up"], 1)
            pool.memset(zero_col[:, :], 0.0).then_inc(S["set_up"], 1)
            pool.wait_ge(S["x_in"], 32)
            for q in range(ADA_FIRST):
                load_ada(q, q, 0)

            def ffn(i, loads):
                g = G[FFNS[i][0]]
                q0 = ADA_FIRST + ADA_FFN * i - 2

                def load_on(n, j, layer):
                    q = q0 + 2 * j + n
                    pool.wait_ge(S["ada_acc"], q - ADA_FIRST // 2 + 1)
                    load_ada(q + 2, n, layer)

                def lo(r, j):
                    slot = (g + r) % SLOTS
                    pool.wait_ge(S["hi_done"], g + r + 3 * j + 1)
                    pool.tensor_tensor(wlo[slot][:, :], raw[slot][:, :], whi[slot][:, :].bitcast(F32), ALU.subtract)\
                        .then_inc(lo_done[slot], 1)

                def pair(j, layer, more=True, first=False):
                    if not first and i in UPS_BY_POOL:
                        lo(1, j)
                    if more and not first and i in GATES_BY_POOL:
                        lo(2, j)
                    if layer is not None:
                        load_on(0, j, layer)
                    if more:
                        lo(3, j)
                    if layer is not None:
                        load_on(1, j, layer)

                for j0, j1, layer in loads:
                    if j1 - j0 > 1:
                        with pool.Fori(j0, j1) as j:
                            pair(j, layer)
                    else:
                        pair(j0, layer, j0 < FP - 1, j0 == 0)

            for q in range(ADA_FIRST, ADA_FIRST + 2):
                pool.wait_ge(S["ada_done"], q - 4)
                load_ada(q, q % 2, 0)
            ffn(0, [(0, 1, None), (1, FP - 1, 0), (FP - 1, FP, 0)])
            second = (ADA_CHUNKS - ADA_FIRST - ADA_FFN) // 2
            ffn(1, [(0, 1, None), (1, second, 0), (second, FP - 1, 1)])
            pool.wait_ge(S["mods_done"], ADA_FIRST + 2 * ADA_FFN)
            pool.wait_ge(S["x_done"], XD["ffn1"])
            pool.dma_start(acol[64:P, 0:1], a["ssd_a_log"].rearrange("o d (h one) -> (o d h) one", one=1))\
                .then_inc(S["ssd_in"], 16)
            pool.dma_start(acol[64:P, 1:2], a["ssd_dt_bias"].rearrange("o d (h one) -> (o d h) one", one=1))\
                .then_inc(S["ssd_in"], 16)
            pool.dma_start(dcol[:, :], a["ssd_d"][0].partition_broadcast(P)).then_inc(S["ssd_in"], 16)
            for i in range(2):
                pool.memset(cpad[i][:, :, :, :], 0.0).then_inc(S["set_up"], 1)
            def lo(c):
                slot = c % SLOTS
                pool.wait_ge(S["hi_done"], c + 1)
                pool.tensor_tensor(wlo[slot][:, :], raw[slot][:, :], whi[slot][:, :].bitcast(F32), ALU.subtract)\
                    .then_inc(lo_done[slot], 1)

            for c in range(G["ssd_in"] + 3, G["ssd_in"] + 15):
                lo(c)
            pool.wait_ge(S["dt_cols"], 1)
            pool.dma_start(q_scratch, q_rows[64:P, :]).then_inc(S["q_stored"], 16)
            pool.wait_ge(S["ssd_in"], 48)
            for t, h0, h1, kept in ((0, 0, 3 * EH, 6), (0, 3 * EH, HEADS, 8), (1, 0, 2 * EH, 8), (1, 2 * EH, HEADS, 8)):
                pool.wait_ge(S["lat_kept"], kept)
                pool.wait_ge(S["state_done"], 2 * (3 + t))
                pool.tensor_tensor(y[:, t, HP * h0:HP * h1].rearrange("p (h q) -> p h q", q=HP),
                                   xl_tok[:, t, HP * h0:HP * h1].rearrange("p (h q) -> p h q", q=HP),
                                   dcol[:, h0:h1].unsqueeze(2).to_broadcast([P, h1 - h0, HP]), ALU.mult)\
                    .then_inc(S["skip_done"], 1)
                if t == 0 and h0 == 0:
                    lo(G["ssd_in"] + 15)
            pool.wait_ge(S["q_stored"], 16)
            for gd in range(2 * GROUPS):
                grp, d = gd // 2, gd % 2
                for part in range(2):
                    if gd == 0:
                        pool.wait_ge(*((S["state_done"], 2 * GROUPS), (S["conv_done"], 12))[part])
                    elif gd == 1:
                        pool.wait_ge(S["off_done"], 4 * GROUPS)
                    else:
                        pool.wait_ge(S["seg_done"], 2 * (gd - 1) + part + 1)
                    h0, row = part * EH // 2, d * HEADS + grp * EH + part * EH // 2
                    pool.dma_start(qb[:, h0:h0 + EH // 2, :] if gd else q_first[part][:, :, :],
                                   q_scratch[row:row + EH // 2, :].partition_broadcast(P))\
                        .then_inc((q_loaded if gd else q_first_loaded)[part], 16)
                if gd >= 2:
                    lo(G["ssd_in"] + 15 + gd)
            pool.wait_ge(S["x_done"], XD["ssd_out"])
            for n in range(2):
                load_ada(ADA_FIRST + 2 * ADA_FFN + n, n, 1)
            pool.dma_start(pool_m[:, :, :], a["pool_tables"].rearrange("g (k p) t -> p (g k) t", p=P))\
                .then_inc(S["pool_in"], 16)
            ffn(2, [(0, 1, None), (1, FP - 1, 1), (FP - 1, FP, 1)])
            ffn(3, [(0, 1, None), (1, LAST_PAIRS, 1), (LAST_PAIRS, FP - 1, None)])
            ffn(4, [(0, 1, None), (1, FP - 1, None)])
            for l in range(DEPTH):
                pool.wait_ge(S["x_done"], XD["final"] if l == 0 else XD["out0"])
                pool.memset(attn[:, :, :, :], 0.0).then_inc(S["attn_zero"], 1)
                pool.wait_ge(S["scan_done"], l + 1)
                for lev, half in enumerate(LEVELS):
                    buf = (qk, scratch)[lev % 2]
                    if lev > 1:
                        pool.wait_ge(S["lev_done"], (NL + 1) * l + lev)
                    hv_, bv = halves(hb, half), halves(buf, half)
                    ref = hv_[:, :, 0, half - 1:half].to_broadcast([P, H2 * T // (2 * half), half])
                    pool.tensor_tensor(bv[:, :, 1, :], hv_[:, :, 1, :], ref, ALU.subtract).then_inc(S["lev_diff"], 1)
                    pool.tensor_tensor(bv[:, :, 0, :], ref, hv_[:, :, 0, :], ALU.subtract).then_inc(S["lev_diff"], 1)
                pool.wait_ge(S["av_done"], 4 * (l + 1))
                for kv in range(2):
                    pool.memset(win[kv][:, :, :, NCMP:16], 0.0).then_inc(S["win_made"], 1)
                    for half in range(2):
                        n0 = CMP_STRIDE * half
                        pos = col("pos_v" if kv else "pos_k")[:, CMP_BLOCK * l + n0:CMP_BLOCK * l + n0 + CMP_STRIDE]
                        src = kvc[:, kv, :, :].rearrange("p g (n b) -> p b g n", b=CMP_STRIDE)[:, :, :, half:half + NCMP]
                        pool.tensor_tensor(win[kv][:, n0:n0 + CMP_STRIDE, :, 0:NCMP], src,
                                           pos.unsqueeze(2).unsqueeze(3).to_broadcast([P, CMP_STRIDE, 2, NCMP]), ALU.add)\
                            .then_inc(S["win_made"], 1)

        @block.tensor
        def _(pe):
            def mm3(out_, wh, wl, xh, xl, start, stop):
                pe.matmul(out_, wh, xh, start=start, stop=False, skip_group_check=True)
                pe.matmul(out_, wh, xl, start=False, stop=False, skip_group_check=True)
                return pe.matmul(out_, wl, xh, start=False, stop=stop, skip_group_check=True)

            def take(c, j=0):
                pe.wait_ge(lo_done[c % SLOTS], c // SLOTS + 1 + j)

            def norm(name, bk=3):
                n = N[name]
                for k in range(KB):
                    pe.wait_ge(S["squares"], KB * n + k + 1)
                    m = pe.matmul(bank[bk][:, 0:T], ones[:, :], scratch[:, k, :], start=k == 0, stop=k == KB - 1)
                m.then_inc(S["stat_done"], 1)

            def ada_chunk(q):
                pe.wait_ge(ada_in[q], 16)
                for blk in range(2):
                    at = 4 * q + 2 * blk
                    for k in range(KB):
                        m = pe.matmul(bank[2][:, at:at + 2], ada[q][:, k, blk * P:(blk + 1) * P], scv[:, k, :],
                                      start=k == 0, stop=k == KB - 1)
                m.then_inc(S["ada_done"], 1)

            def ada_sums(q, slot, vectors, acc=None):
                pe.wait_ge(S["ada_acc"], q - ADA_FIRST // 2 + 1 if acc is None else acc)
                if slot == 0:
                    pe.wait_ge(S["mods_done"], q)
                sums_ = ada_acc[slot if acc is None else (acc + 1) % 2]
                for blk in range(2):
                    for v in range(vectors):
                        at = 4 * slot + 2 * blk + v
                        m = pe.matmul(bank[2][:, at:at + 1], sums_[:, v, blk * P:(blk + 1) * P], ones[:, 0:1],
                                      start=True, stop=True)
                m.then_inc(S["ada_done"], 1)

            def project(c, bk, uh, ul, u_from=None):
                take(c)
                wh, wl = chunk(c, KB, 256)
                for blk in range(2):
                    f = slice(blk * P, (blk + 1) * P)
                    for k in range(KB):
                        if u_from is not None and blk == 0:
                            pe.wait_ge(S["u_done"], u_from + k + 1)
                        m = mm3(bank[bk][:, blk * T:(blk + 1) * T], wh[:, k, f], wl[:, k, f], uh[:, k, :], ul[:, k, :],
                                k == 0, k == KB - 1)
                return m

            def project_tokens(c, bk, n):
                take(c)
                wh, wl = chunk(c, KB, n)
                for tile in range(TT):
                    t = slice(tile * P, (tile + 1) * P)
                    for k in range(KB):
                        m = mm3(bank[bk][:, tile * n:(tile + 1) * n], u_hi[:, k, t], u_lo[:, k, t], wh[:, k, :],
                                wl[:, k, :], k == 0, k == KB - 1)
                return m

            def ffn(i, beside=None):
                name, l, s = FFNS[i]
                g = G[name]
                uh, ul = (uc_hi, uc_lo) if i == 0 else (u_hi, u_lo)
                q0 = ADA_FIRST + ADA_FFN * i
                pairs = FP * i

                def hidden(c, bk, u_from=None, j=0):
                    take(c, j)
                    wh, wl = chunk(c, KB, 256)
                    for blk in range(2):
                        f = slice(blk * P, (blk + 1) * P)
                        for k in range(KB):
                            if u_from is not None and blk == 0:
                                pe.wait_ge(S["u_done"], u_from + k + 1)
                            m = mm3(bank[bk][:, blk * T:(blk + 1) * T], wh[:, k, f], wl[:, k, f], uh[:, k, :],
                                    ul[:, k, :], k == 0, k == KB - 1)
                    m.then_inc(S["chunk_used"], 1)

                def down(c, opens, closes, j=0):
                    take(c, j)
                    wh, wl = chunk(c, 2, D)
                    for b in range(KB):
                        f = slice(b * P, (b + 1) * P)
                        for kk in range(2):
                            m = mm3(bank[4 + b // 2][:, (b % 2) * T:(b % 2 + 1) * T], wh[:, kk, f], wl[:, kk, f],
                                    h_hi[:, kk, :], h_lo[:, kk, :], opens and kk == 0 and b % 2 == 0,
                                    closes and kk == 1)
                        if closes and b in (1, 3, 5):
                            m.then_inc(S["y_done"], 1)
                    m.then_inc(S["chunk_used"], 1)

                def pair(j, q, opens, vectors):
                    pe.wait_ge(S["silu_done"], pairs + j)
                    hidden(g + 2, 0, None, j - 1)
                    pe.wait_ge(S["h_done"], pairs + j)
                    down(g + 3, opens, False, j - 1)
                    if vectors:
                        ada_sums(q, 0, vectors)
                    pe.wait_ge(S["mult_done"], pairs + j)
                    hidden(g + 4, 1, None, j - 1)
                    if vectors:
                        ada_sums(q + 1, 1, vectors)

                pe.wait_ge(S["x_done"], XD[["load", "ffn0", "ssd_out", "ffn2", "pool"][i]])
                if pairs:
                    pe.wait_ge(S["silu_done"], pairs)
                hidden(g, 0, 8 * NSP[["ctx_f0", "lat_f0", "lat_f1", "l1_f0", "l1_f1"][i]])
                if beside:
                    beside()
                if pairs:
                    pe.wait_ge(S["mult_done"], pairs)
                hidden(g + 1, 1)
                for j0, j1, vectors in ADA_PAIRS[i]:
                    if j0 == 1:
                        pair(1, q0, True, vectors)
                    with pe.Fori(max(j0, 2), j1) as j:
                        pair(j, q0 + 2 * (j - 1), False, vectors)
                pe.wait_ge(S["h_done"], pairs + FP)
                down(g + 3 * FP - 1, False, True)

            pe.wait_ge(S["consts_in"], 16)
            pe.wait_ge(S["rows_in"], 16 * len(ROWS))
            for t in range(ROW_TILES):
                n = P if t < ROW_TILES - 1 else LAST_ROWS
                dst = bank[t // 4][:, (t % 4) * P:(t % 4) * P + n]
                pe.transpose(dst, rows[0:n, t, :], ident[0:n, 0:n]).then_inc(S["cols_turned"], 1)
            pe.wait_ge(S["x_in"], 32)
            for stream in range(2):
                for pr in range(KB // 2):
                    if stream:
                        pe.wait_ge(S["x_done"], pr + 1)
                    for kk in range(2):
                        for tile in range(TT):
                            k = 2 * pr + kk
                            m = pe.transpose(bank[4 + pr][:, kk * T + tile * P:kk * T + (tile + 1) * P],
                                             x_in[stream][:, tile, k * P:(k + 1) * P], ident)
                    m.then_inc(S["x_turned"], 1)
            pe.wait_ge(S["set_up"], 3)
            norm("ctx_f0")
            pe.wait_ge(S["cols_done"], 2)
            norm("lat_f0", 1)
            pe.wait_ge(S["silu_c"], 2)
            ada_chunk(0)
            for q in range(2, ADA_FIRST, 2):
                ada_chunk(q)
                ada_sums(q - 1, q - 1, 2, q // 2)
            ada_sums(ADA_FIRST - 1, ADA_FIRST - 1, 2, ADA_FIRST // 2)
            pe.wait_ge(S["root_done"], 2)
            ffn(0)
            ffn(1, lambda: norm("ctx_ssd"))

            norm("lat_ssd")
            c0 = G["ssd_in"]
            take(c0)
            wh, wl = chunk(c0, KB, P)
            for s, (uh, ul) in enumerate(((u_hi, u_lo), (uc_hi, uc_lo))):
                for k in range(KB):
                    if s == 0:
                        pe.wait_ge(S["u_done"], 8 * NSP["lat_ssd"] + k + 1)
                    m = mm3(bank[2][:, s * T:(s + 1) * T], wh[:, k, :], wl[:, k, :], uh[:, k, :], ul[:, k, :],
                            k == 0, k == KB - 1)
            m.then_inc(S["chunk_used"], 1)

            def xbc(i):
                if i >= 2:
                    pe.wait_ge(S["conv_in"], CONV_IN[i - 2])
                m = project(c0 + 1 + i, 4 + 2 * (i % 2), u_hi, u_lo)
                if i not in (2, 3):
                    m = project(c0 + 1 + i, 5 + 2 * (i % 2), uc_hi, uc_lo)
                m.then_inc(S["chunk_used"], 1)

            def turn(i):
                xi = i - 4
                pe.wait_ge(S["conv_silu"], CONV_SILU[i])
                if xi == 0:
                    pe.wait_ge(S["tok_done"], 1)
                if xi > 0:
                    pe.wait_ge(S["lat_kept"], xi)
                for s in ((1,) if i < 2 else (0, 1)):
                    if s == 1:
                        if i == 0:
                            pe.wait_ge(S["dt_taken"], 1)
                        else:
                            pe.wait_ge(S["ctx_kept"], 1 if i == 1 else 2 + 2 * xi)
                    for tile in range(TT):
                        for blk in range(2):
                            m = pe.transpose(bank[3 - s][:, (2 * tile + blk) * P:(2 * tile + blk + 1) * P],
                                             xsil[:, blk, s, tile * P:(tile + 1) * P], ident)
                    m.then_inc(S["turned"], 1)

            def states(g):
                pe.wait_ge(S["ctx_kept"], 6 + 4 * g)
                for d in range(2):
                    if g:
                        pe.wait_ge(S["state_kept"], 2 * g - 1 + d)
                    for tile in range(TT):
                        m = pe.matmul(bank[d][:, :], Bc_tok[:, tile, g * NS:(g + 1) * NS], xw[g % 2][:, d, tile, :],
                                      start=tile == 0, stop=tile == TT - 1)
                    m.then_inc(S["state_done"], 1)

            for i in range(12):
                xbc(i)
                if i == 2:
                    turn(0)
                if i == 3:
                    pe.wait_ge(S["dt_cols"], 4)
                    pe.wait_ge(S["dt_exp"], 4)
                    for which, slab in enumerate((q_rows, dtt[0], dtt[5], dtt[6])):
                        for tile in range(TT):
                            at = (which * TT + tile) * 64
                            m = pe.transpose(bank[3][:, at:at + 64], slab[64:P, tile * P:(tile + 1) * P],
                                             ident[64:P, 64:P])
                    m.then_inc(S["tok_turned"], 1)
                    turn(1)
                if i >= 5:
                    turn(i - 1)
                if i in (7, 9, 11):
                    states((i - 7) // 2)

            def z_chunk(z):
                if z >= 3:
                    pe.wait_ge(S["z_kept"], z - 2)
                elif z == 0:
                    pe.wait_ge(S["conv_in"], CONV_IN[11])
                project_tokens(c0 + 13 + z, 4 + z % 3, 256).then_inc(S["chunk_used"], 1)

            z_chunk(0)
            turn(11)
            states(3)
            pe.wait_ge(S["state_kept"], 2 * GROUPS)
            pe.wait_ge(S["lat_kept"], 8)
            n = 0
            for tile in range(TT):
                for g in range(GROUPS):
                    for d in range(2):
                        if n >= 4:
                            pe.wait_ge(S["off_added"], n - 3)
                        pe.matmul(bank[n % 4][:, :], CT[:, g, tile * P:(tile + 1) * P], hc[:, d, g, :],
                                  start=True, stop=True).then_inc(S["off_done"], 1)
                        n += 1
            pe.wait_ge(S["off_added"], n)

            def b_dot_c(g):
                if g:
                    pe.wait_ge(S["cb_kept"], g)
                for tile in range(TT):
                    m = pe.matmul(bank[2][:, tile * T:(tile + 1) * T], BT[:, g, tile * P:(tile + 1) * P],
                                  CT[:, g, :], start=True, stop=True)
                m.then_inc(S["cb_done"], 1)

            b_dot_c(0)
            for gd in range(2 * GROUPS):
                g, d = gd // 2, gd % 2
                if d and gd < 7:
                    b_dot_c(g + 1)
                if gd < 7:
                    z_chunk(gd + 1)
                if d == 0 and g >= 2:
                    pe.wait_ge(S["y_added"], 2 * (g - 1))
                for h in range(EH):
                    if h % (EH // 2) == 0:
                        pe.wait_ge(S["m_done"], 2 * gd + h // (EH // 2) + 1)
                    for key, m_, parts in ((d, e_long[d], (0, 1)), (1 - d, e_short[d], (1 - d,))):
                        for lt in parts:
                            lhs = m_[:, h, lt * P:(lt + 1) * P] if m_ is e_long[d] else m_[:, h, :]
                            m = pe.matmul(bank[DIAG_BANKS[g % 2][lt]][:, h * HP:(h + 1) * HP], lhs,
                                          xl_tok[:, key, (g * EH + h) * HP:(g * EH + h + 1) * HP],
                                          start=d == 0 and h == 0 and m_ is e_long[d], stop=d == 1,
                                          skip_group_check=True)
                m.then_inc(S["diag_done"], 1)
            pe.wait_ge(S["z_kept"], 8)
            for u in range(INNER // P // 2):
                g = u // 2
                if u % 2 == 0:
                    pe.wait_ge(S["g_norm"], 2 * (g + 1))
                if u >= 4:
                    pe.wait_ge(S["g_ready"], 2 * (u - 3))
                if u == 0:
                    pe.wait_ge(S["y_added"], 2 * (GROUPS - 1))
                for kk in range(2):
                    for tile in range(TT):
                        k = 2 * u + kk
                        m = pe.transpose(bank[G_BANKS[u % 4]][:, kk * T + tile * P:kk * T + (tile + 1) * P],
                                         y[:, tile, k * P:(k + 1) * P], ident)
                m.then_inc(S["g_turned"], 1)
            pe.wait_ge(S["y_added"], 2 * GROUPS)

            def out_chunk(c, o, kh, bk, hi, lo):
                take(c)
                wh, wl = chunk(c, KB, 256)
                for blk in range(2):
                    f = slice(blk * P, (blk + 1) * P)
                    for k in range(KB):
                        m = mm3(bank[bk][:, blk * T:(blk + 1) * T], wh[:, k, f], wl[:, k, f], hi[:, 8 * kh + k, :],
                                lo[:, 8 * kh + k, :], kh == 0 and blk == 0 and k == 0, kh == 1 and k == KB - 1)
                m.then_inc(S["chunk_used"], 1)

            for o in range(4):
                for kh in range(2):
                    pe.wait_ge(S["g_ready"], 8 * (kh + 1))
                    if o == 3 and kh == 0:
                        pe.wait_ge(S["x_done"], XD["ffn1"] + 2)
                    out_chunk(G["ssd_out"] + 2 * o + kh, o, kh, 5 + o % 3, g_hi, g_lo)

            norm("lat_f1")
            ffn(2)
            norm("l1_f0")
            ffn(3)

            norm("l1_pool")
            c = G["pool"]
            take(c)
            wh, wl = chunk(c, KB, 256)
            for g in range(len(WINDOWS)):
                pe.wait_ge(S["u_done"], 8 * NSP["l1_pool"] + 2 * g + 2)
                for tile in range(TT):
                    t = slice(tile * P, (tile + 1) * P)
                    for k in range(2):
                        m = mm3(bank[4 + g][:, tile * T:(tile + 1) * T], u_hi[:, 2 * g + k, t], u_lo[:, 2 * g + k, t],
                                wh[:, 2 * g + k, :], wl[:, 2 * g + k, :], k == 0, k == 1)
                if g < len(WINDOWS) - 1:
                    m.then_inc(S["pool_first"], 1)
            m.then_inc(S["chunk_used"], 1)
            pe.wait_ge(S["pool_in"], 16)
            pe.wait_ge(S["root_done"], N["l1_pool"] + 1)
            for g in range(len(WINDOWS)):
                pe.wait_ge(S["pool_kept"], g + 1)
                for db in range(2):
                    for tile in range(TT):
                        m = pe.matmul(bank[g][:, db * T:(db + 1) * T], pq[:, tile, g, db * P:(db + 1) * P],
                                      pool_m[:, 2 * g + tile, :], start=tile == 0, stop=tile == TT - 1)
                m.then_inc(S["pool_done"], 1)
            norm("l1_f1", 4)
            ffn(4)
            norm("final")

            def level(l, i):
                if i < 0:
                    pe.wait_ge(S["scan_done"], l + 1)
                    pe.wait_ge(S["hgrn_step_a"], 3 + 5 * l)
                    pe.wait_ge(S["proj_kept"], NP_ * l + 8)
                else:
                    pe.wait_ge(S["lev_ready"], NL * l + i + 1)
                    if i == 1:
                        pe.wait_ge(S["off_kept"], 2 * (l + 1))
                    pe.wait_ge(S["lev_kept"], 4 * (NL * l + max(i, 1)))
                if i == 0:
                    for h in range(H2):
                        m = pe.matmul(bank[h // 4][:, (h % 4) * P:(h % 4 + 1) * P], qk[:, h, 0:P], qk[:, h, P:T],
                                      start=True, stop=True)
                else:
                    ka, qa = (hk, hq) if i < 0 else (((qk, scratch)[i % 2]),) * 2
                    for un in range(H2 * TT):
                        h, tile = un // TT, un % TT
                        t = slice(tile * P, (tile + 1) * P)
                        m = pe.matmul(bank[un // 4][:, (un % 4) * P:(un % 4 + 1) * P], ka[:, h, t], qa[:, h, t],
                                      start=True, stop=True)
                m.then_inc(S["lev_done"], 1)

            def score(l, br, s):
                n = 12 * l + 6 * br + s
                ps = bank[s % 2]
                if n >= 2:
                    pe.wait_ge(S["score_exp"], n - 1)
                if s < 2:
                    pe.matmul(ps[:, :].rearrange("p (h s) -> p h s", h=4), ident,
                              causal.unsqueeze(1).to_broadcast([P, 4, P]), start=True, stop=False,
                              skip_group_check=True)
                    for hh in range(4):
                        m = pe.matmul(ps[:, hh * P:(hh + 1) * P], nq[:, 4 * s + hh, 0:P], ksw[:, br, s, 0:P],
                                      start=False, stop=True, skip_group_check=True)
                else:
                    h0 = 2 * (s - 2)
                    for hh in range(2):
                        pe.matmul(ps[:, hh * T:(hh + 1) * T], nq[:, h0 + hh, P:T], ksw[:, br, h0 // 4, :],
                                  start=hh == 0, stop=False, skip_group_check=True)
                    m = pe.matmul(ps[:, :].rearrange("p (h s) -> p h s", h=2)[:, :, P:T], ident,
                                  causal.unsqueeze(1).to_broadcast([P, 2, P]), start=False, stop=True,
                                  skip_group_check=True)
                m.then_inc(S["score_done"], 1)

            def turn_probs(l, br, n):
                nb = 2 * l + br
                part, half = TURNS[n]
                pe.wait_ge(S["prob_done"], 3 * nb + (1, 1, 2, 2, 3, 3)[n])
                if n >= 2 or nb:
                    pe.wait_ge(S[("p_kept_a", "p_kept_v")[n % 2]], 3 * nb + n // 2)
                for hh in range(4):
                    h = 4 * half + hh
                    src = (pr0[:, h, :], pr1[:, h, 0:P], pr1[:, h, P:T])[part]
                    m = pe.transpose(bank[2 + n % 2][:, hh * P:(hh + 1) * P], src, ident)
                m.then_inc(S["p_turned"], 1)

            def weigh_values(l, br):
                nb = 2 * l + br
                pe.wait_ge(S["p_kept_a"], 3 * (nb + 1))
                pe.wait_ge(S["p_kept_v"], 3 * (nb + 1))
                for hp in range(4):
                    f = slice(hp // 2 * P, (hp // 2 + 1) * P)
                    pe.matmul(bank[4 + hp][:, :], vsw[:, br, 0, f], pt0[:, 2 * hp:2 * hp + 2, :], start=False,
                              stop=False, skip_group_check=True)
                    pe.matmul(bank[4 + hp][:, :].rearrange("p (h t) -> p h t", h=2)[:, :, P:T], vsw[:, br, 1, f],
                              pt1[:, 2 * hp:2 * hp + 2, :], start=False, stop=br == 1, skip_group_check=True)\
                        .then_inc(S["av2_done"], 1)

            def compress(l, i):
                c, kv = G[f"cmp{l}"] + i, i // 2
                take(c)
                pe.wait_ge(S["win_done"], 2 * l + kv + 1)
                if i % 2 == 0:
                    pe.wait_ge(S["proj_kept"], NP_ * l + 29 + kv)
                wh, wl = chunk(c, CMP_BLOCK // 2, P)
                for n in range(CMP_BLOCK // 2):
                    at = (i % 2) * (CMP_BLOCK // 2) + n
                    m = mm3(bank[5 + kv][:, 0:32], wh[:, n, :], wl[:, n, :], win_hi[kv][:, at, :, :],
                            win_lo[kv][:, at, :, :], at == 0, at == CMP_BLOCK - 1)
                m.then_inc(S["chunk_used"], 1)

            def rope(l, r):
                src = ksw[0:ROT, r, :, :] if r < 2 else nq[0:ROT, 2 * (r - 2):2 * (r - 2) + 2, :]
                pe.wait_ge(S["proj_kept"], NP_ * l + (15, 16, 19, 20, 21, 22)[r])
                if r or l:
                    pe.wait_ge(S["rope_done"], 6 * l + r)
                pe.matmul(bank[7][0:ROT, :], rot, src, start=True, stop=True).then_inc(S["roped"], 1)

            pe.wait_ge(S["w2_in"], 64)
            for l in range(DEPTH):
                norm(f"pre{l}")
                g = G[f"proj{l}"]
                kept = NP_ * l
                for i, (_c, n, tok) in enumerate(PROJ):
                    if i >= 3:
                        pe.wait_ge(S["proj_kept"], kept + i - 2)
                    if tok:
                        m = project_tokens(g + i, 4 + i % 3, n)
                    else:
                        m = project(g + i, 4 + i % 3, u_hi, u_lo, None if i else 8 * NSP[f"pre{l}"])
                    m.then_inc(S["chunk_used"], 1)
                    for lev in range(len(LEVELS)):
                        if i == LEVEL_AT(lev):
                            level(l, lev)
                    if i == DIAG_AT:
                        level(l, -1)
                    for r in range(6):
                        if i == ROPE_AT[r]:
                            rope(l, r)
                    if i == AV_AT:
                        pe.wait_ge(S["lev_kept"], 4 * len(LEVELS) * (l + 1))
                        for h in range(H2):
                            o = bank[h // 2][:, (h % 2) * T:(h % 2 + 1) * T]
                            v0, v1 = hv[:, 0, h * P:(h + 1) * P], hv[:, 1, h * P:(h + 1) * P]
                            pe.matmul(o[:, 0:P], v0, attn[:, h, 0, :], start=True, stop=True)
                            pe.matmul(o[:, P:T], v0, attn_off[:, h, :], start=True, stop=False)
                            m = pe.matmul(o[:, P:T], v1, attn[:, h, 1, :], start=False, stop=True)
                            if h % 2:
                                m.then_inc(S["av_done"], 1)
                    if i == AV_AT + 1:
                        pe.wait_ge(S["o_sq"], 4 * (l + 1))
                        pe.wait_ge(S["rope_done"], 6 * (l + 1))
                        for un in range(H2 * TT):
                            h, tile = un // TT, un % TT
                            m = pe.matmul(bank[7][:, un:un + 1], scratch[:, h, tile * P:(tile + 1) * P], ones[:, 0:1],
                                          start=True, stop=True)
                        m.then_inc(S["o_stat"], 1)
                    if i == AV_AT + 2:
                        pe.wait_ge(S["o_recip"], l + 1)
                        pe.wait_ge(S["o_kept"], 4 * (l + 1))
                        for un in range(H2 * TT):
                            m = pe.matmul(bank[un // 4][:, (un % 4) * P:(un % 4 + 1) * P],
                                          small[:, 32 + un:33 + un].to_broadcast([P, P]), ident, start=True, stop=True)
                            if un % 4 == 3:
                                m.then_inc(S["o_rstd"], 1)
                pe.wait_ge(S["o_gated"], 4 * (l + 1))
                compress(l, 0)
                compress(l, 1)
                score(l, 0, 0)
                score(l, 0, 1)
                pe.wait_ge(S["cmp_silu"], 2 * l + 1)
                pe.wait_ge(S["o_root"], l + 1)
                pe.matmul(bank[7][:, 0:32], w2[:, l, 0, :], hid[:, :, :], start=True, stop=True)\
                    .then_inc(S["cmp_out"], 1)
                compress(l, 2)
                score(l, 0, 2)
                score(l, 0, 3)
                pe.wait_ge(S["cmp_kept"], 2 * l + 1)
                pe.matmul(bank[7][0:ROT, 64:96], rot, kcmp[0:ROT, :, :], start=True, stop=True)\
                    .then_inc(S["cmp_rot"], 1)
                compress(l, 3)
                score(l, 0, 4)
                score(l, 0, 5)
                pe.wait_ge(S["cmp_silu"], 2 * l + 2)
                for g2 in range(2):
                    m = pe.matmul(bank[5][0:16, g2 * P:(g2 + 1) * P], hid[:, g2, :], w2[:, l, 1, :],
                                  start=True, stop=True)
                m.then_inc(S["cmp_out"], 1)
                pe.wait_ge(S["cmp_ready"], l + 1)
                pe.wait_ge(S["score_exp"], 12 * l + 5)
                for tile in range(TT):
                    pe.matmul(bank[0][:, tile * P:(tile + 1) * P].rearrange("p (h n) -> p h n", n=16), ident,
                              cmp_mask[tile].unsqueeze(1).to_broadcast([P, H2, 16]), start=True, stop=False,
                              skip_group_check=True)
                    for h in range(H2):
                        m = pe.matmul(bank[0][:, tile * P + 16 * h:tile * P + 16 * h + 16],
                                      nq[:, h, tile * P:(tile + 1) * P], kcmp[:, h // 4, :], start=False, stop=True,
                                      skip_group_check=True)
                m.then_inc(S["c_score"], 1)
                turn_probs(l, 0, 0)
                turn_probs(l, 0, 1)
                pe.wait_ge(S["c_diff"], l + 1)
                score(l, 1, 0)
                score(l, 1, 1)
                pe.wait_ge(S["c_prob"], l + 1)
                for hp in range(4):
                    if hp < 2:
                        pe.wait_ge(S[("p_kept_a", "p_kept_v")[hp]], 6 * l + 1)
                    else:
                        pe.wait_ge(S["c_kept"], 4 * l + hp - 1)
                    for hh in range(2):
                        for tile in range(TT):
                            m = pe.transpose(bank[2 + hp % 2][0:16, hh * T + tile * P:hh * T + (tile + 1) * P],
                                             prc[:, tile, 2 * hp + hh, :], ident)
                    m.then_inc(S["c_turned"], 1)
                pe.wait_ge(S["cmp_kept"], 2 * l + 2)
                pe.wait_ge(S["proj_kept"], kept + NP_)
                for hp in range(4):
                    pe.wait_ge(S["c_kept"], 4 * l + hp + 1)
                    pe.matmul(bank[4 + hp][:, :], vcmp[0:16, hp // 2, :], ptc[0:16, 2 * hp:2 * hp + 2, :],
                              start=True, stop=False, skip_group_check=True)
                for n in range(2, 6):
                    turn_probs(l, 0, n)
                score(l, 1, 2)
                score(l, 1, 3)
                weigh_values(l, 0)
                score(l, 1, 4)
                score(l, 1, 5)
                for n in range(6):
                    turn_probs(l, 1, n)
                weigh_values(l, 1)
                for o in range(4):
                    for kh in range(2):
                        pe.wait_ge(S["fin_done"], 8 * l + 4 * (kh + 1))
                        if o < 3 and kh == 0:
                            pe.wait_ge(S["score_exp"], 12 * (l + 1))
                            pe.wait_ge(S["p_kept_a"], 6 * (l + 1))
                        if o == 3 and kh == 0:
                            pe.wait_ge(S["squares"], 8 * N[f"post{l}"] + 2)
                        out_chunk(G[f"out{l}"] + 2 * o + kh, o, kh, o % 3, fin_hi, fin_lo)
                norm(f"post{l}")
            pe.wait_ge(S["x_done"], XD["out1"])
            for tile in range(TT):
                for half in range(2):
                    for k in range(4):
                        m = pe.transpose(bank[4 + 2 * tile + half][:, k * P:(k + 1) * P],
                                         x[:, 4 * half + k, tile * P:(tile + 1) * P], ident)
                    m.then_inc(S["x_out_turned"], 1)

        @block.scalar
        def _(act):
            def hi(c, slot, loads, n=CH, first=False):
                act.wait_ge(landed[slot], 16 * loads)
                if not first:
                    act.wait_ge(S["chunk_used"], c - 2)
                nc.scalar.activation(whi[slot][:, 0:n], raw[slot][:, 0:n], ACT.Copy).then_inc(S["hi_done"], 1)

            def hi_at(c):
                if c < CHUNKS:
                    hi(c, c % SLOTS, c // SLOTS + 1, CHUNK_FLOATS.get(c, CH), c < SLOTS)

            def squares(name, src, ready):
                if name not in ("ctx_f0", "lat_f0", "ctx_ssd"):
                    nc.scalar.activation(root_table[:, :], zero_col[:, :], ACT.Sqrt)
                for k in range(KB):
                    act.wait_ge(S["x_done"], ready(k))
                    nc.scalar.activation(scratch[:, k, :], src[:, k, :], ACT.Square).then_inc(S["squares"], 1)

            def after(stage):
                return lambda k: XD[stage] - KB + k + 1

            def root(name, bk=3):
                n = N[name]
                act.wait_ge(S["stat_done"], n + 1)
                nc.scalar.activation(rms[n % 2][:, :], bank[bk][:, 0:T], ACT.Sqrt, bias=EPS, scale=1.0 / D)\
                    .then_inc(S["root_done"], 1)

            def rounded(name, dst, shift):
                for k in range(KB):
                    act.wait_ge(S["scaled"], 8 * NSC[name] + k + 1)
                    nc.scalar.activation(dst[:, k, :], scratch[:, k, :], ACT.Identity, bias=shift(k))\
                        .then_inc(S["u_hi_done"], 1)

            def shifted(l, s, v):
                return lambda k: mods[l][:, 8 * 3 * s + k, v:v + 1]

            def ffn(i, beside=None):
                g = G[FFNS[i][0]]
                pairs = FP * i

                def hi_r(c, r, j, n_before):
                    hi(c, (g + r) % SLOTS, (g + r) // SLOTS + 1 + j, CH)

                def silu(j, c):
                    act.wait_ge(S["chunk_used"], c + 1)
                    nc.scalar.activation(hs[:, :], bank[0][:, :], ACT.Silu).then_inc(S["silu_done"], 1)

                def h_rounded(j):
                    act.wait_ge(S["mult_done"], pairs + j)
                    nc.scalar.activation(h_hi[:, :, :].rearrange("p k t -> p (k t)"), hf[:, :], ACT.Copy)\
                        .then_inc(S["h_hi_done"], 1)

                hi_at(g + 2)
                silu(0, g)
                hi_at(g + 3)
                if beside:
                    beside()
                with act.Fori(1, FP - 1) as j:
                    h_rounded(j)
                    hi_r(g + 3 * j + 1, 1, j, 0)
                    silu(j, g + 3 * j - 1)
                    hi_r(g + 3 * j + 2, 2, j, 0)
                    hi_r(g + 3 * j + 3, 3, j, 0)
                h_rounded(FP - 1)
                hi_at(g + 3 * FP - 2)
                silu(FP - 1, g + 3 * FP - 4)
                hi_at(g + 3 * FP - 1)
                h_rounded(FP)
                hi_at(g + 3 * FP)
                hi_at(g + 3 * FP + 1)

            act.dma_start(consts[:, :], a["shape_consts"]).then_inc(S["consts_in"], 16)
            act.dma_start(x_in[0][:, :, :], a["ctx"][0].rearrange("(i p) d -> p i d", p=P)).then_inc(S["x_in"], 16)
            act.dma_start(x_in[1][:, :, :], a["x"][0].rearrange("(i p) d -> p i d", p=P)).then_inc(S["x_in"], 16)
            act.dma_start(mask_in[:, :, :], a["level_masks"].rearrange("p (i t) -> p i t", t=P))\
                .then_inc(S["mask_in"], 16)
            for l in range(DEPTH):
                for i, name in enumerate(("cmp_w2_k_2", "cmp_w2_v_2")):
                    act.dma_start(w2[:, l, i, :], a[name][l]).then_inc(S["w2_in"], 16)
            act.wait_ge(S["cols_done"], 2)
            nc.scalar.activation(scv[:, :, 0], col("c"), ACT.Silu).then_inc(S["silu_c"], 1)
            nc.scalar.activation(scv[:, :, 1], col("c_ctx"), ACT.Silu).then_inc(S["silu_c"], 1)
            squares("ctx_f0", xc, lambda k: k // 2 + 1)
            root("ctx_f0")
            squares("lat_f0", x, lambda k: 5 + k // 2)
            root("lat_f0", 1)
            hi_at(0)
            hi_at(1)
            rounded("ctx_f0", uc_hi, shifted(0, 0, 1))
            rounded("lat_f0", u_hi, shifted(0, 0, 0))
            ffn(0)
            squares("ctx_ssd", xc, after("ffn0"))

            def ctx_norm():
                root("ctx_ssd")
                rounded("ctx_ssd", uc_hi, shifted(0, 1, 1))

            ffn(1, ctx_norm)

            squares("lat_ssd", x, after("ffn1"))
            root("lat_ssd")
            rounded("lat_ssd", u_hi, shifted(0, 1, 0))
            c0 = G["ssd_in"]
            hi_at(c0 + 2)
            R = slice(64, P)
            act.wait_ge(S["dt_taken"], 2)
            nc.scalar.activation(dtt[2][R, :], dtt[1][R, :], ACT.Exp).then_inc(S["dt_exp"], 1)
            act.wait_ge(S["ssd_in"], 48)
            nc.scalar.activation(acol[R, 2:3], acol[R, 0:1], ACT.Exp).then_inc(S["dt_exp"], 1)
            hi_at(c0 + 3)
            act.wait_ge(S["dt_cols"], 2)
            nc.scalar.activation(dtt[5][R, 0:T], q_rows[R, :], ACT.Exp, bias=acol[R, 3:4]).then_inc(S["dt_exp"], 1)
            act.wait_ge(S["dt_cols"], 3)
            nc.scalar.activation(dtt[2][R, 0:T], dtt[4][R, 0:T], ACT.Exp).then_inc(S["dt_exp"], 1)

            def lat_keep(xi):
                act.wait_ge(S["turned"], 3 + 2 * xi)
                nc.scalar.activation(xl_tok[:, :, 256 * xi:256 * xi + 256],
                                     bank[3][:, :].rearrange("p (t n) -> p t n", t=TT), ACT.Copy)\
                    .then_inc(S["lat_kept"], 1)

            def state_keep(g):
                for d in range(2):
                    act.wait_ge(S["state_done"], 2 * g + d + 1)
                    nc.scalar.activation(hc[:, d, g, :], bank[d][:, :], ACT.Copy).then_inc(S["state_kept"], 1)

            for i in range(12):
                c = c0 + 1 + i
                if i == 0:
                    act.wait_ge(S["set_up"], 5)
                act.wait_ge(S["chunk_used"], c + 1)
                if i >= 2:
                    act.wait_ge(S["conv_done"], i - 1)
                for s in ((0, 1) if i not in (2, 3) else (0,)):
                    nc.scalar.activation(cpad[i % 2][:, :, s, PAD:PAD + T],
                                         bank[4 + s + 2 * (i % 2)][:, :].rearrange("p (b t) -> p b t", b=2),
                                         ACT.Copy).then_inc(S["conv_in"], 1)
                hi_at(c + 3)
                if i >= 5:
                    lat_keep(i - 5)
                act.wait_ge(S["conv_done"], i + 1)
                if i >= 5:
                    act.wait_ge(S["turned"], 2 * (i - 4) + 2)
                elif i == 1:
                    act.wait_ge(S["turned"], 1)
                elif i == 4:
                    act.wait_ge(S["turned"], 2)
                if i < 2:
                    nc.scalar.activation(BT[:, 2 * i:2 * i + 2, :], cacc[:, :, 0, :], ACT.Silu)\
                        .then_inc(S["conv_silu"], 1)
                    nc.scalar.activation(xsil[:, :, 1, :], cacc[:, :, 1, :], ACT.Silu).then_inc(S["conv_silu"], 1)
                elif i < 4:
                    nc.scalar.activation(CT[:, 2 * i - 4:2 * i - 2, :], cacc[:, :, 0, :], ACT.Silu)\
                        .then_inc(S["conv_silu"], 1)
                else:
                    nc.scalar.activation(xsil[:, :, :, :], cacc[:, :, :, :], ACT.Silu).then_inc(S["conv_silu"], 1)
                if i in (7, 9, 11):
                    state_keep((i - 7) // 2)

            def z_keep(z):
                act.wait_ge(S["chunk_used"], c0 + 14 + z)
                nc.scalar.activation(sz[:, :, 256 * z:256 * z + 256],
                                     bank[4 + z % 3][:, :].rearrange("p (t n) -> p t n", t=TT), ACT.Silu)\
                    .then_inc(S["z_kept"], 1)
                hi_at(c0 + 13 + z + 3)

            z_keep(0)
            lat_keep(7)
            state_keep(3)
            def group_squares(g):
                for tile in range(TT):
                    un = 2 * g + tile
                    act.wait_ge(S["gated"], un + 1)
                    if un:
                        act.wait_ge(S["act_step"], un)
                    nc.scalar.activation(sq_dump[:, tile, :], y[:, tile, 512 * g:512 * g + 512], ACT.Square,
                                         accum_out=small[:, 16 + un:17 + un]).then_inc(S["act_step"], 1)

            def group_roots(g0, g1):
                act.wait_ge(S["act_step"], 2 * g1)
                nc.scalar.activation(small[:, 24 + 2 * g0:24 + 2 * g1], small[:, 16 + 2 * g0:16 + 2 * g1], ACT.Sqrt,
                                     bias=EPS, scale=1.0 / 512).then_inc(S["g_root"], 1)

            def g_rounded(u):
                act.wait_ge(S["g_turned"], u + 1)
                for kk in range(2):
                    k = 2 * u + kk
                    nc.scalar.activation(g_hi[:, k, :], bank[G_BANKS[u % 4]][:, kk * T:(kk + 1) * T], ACT.Identity,
                                         scale=col("ssd_norm")[:, k:k + 1], bias=0.0).then_inc(S["g_hi_kept"], 1)

            for gd in range(2 * GROUPS):
                g, d = gd // 2, gd % 2
                for part in range(2):
                    act.wait_ge(S["seg_done"], 2 * gd + part + 1)
                    hs_ = slice(part * EH // 2, (part + 1) * EH // 2)
                    nc.scalar.activation(e_long[d][:, hs_, :], e_long[d][:, hs_, :], ACT.Exp)
                    nc.scalar.activation(e_short[d][:, hs_, :], e_short[d][:, hs_, :], ACT.Exp)\
                        .then_inc(S["e_done"], 1)
                if d == 0:
                    act.wait_ge(S["cb_done"], g + 1)
                    if g:
                        act.wait_ge(S["m_done"], 4 * g)
                    nc.scalar.activation(cb[:, :, :].rearrange("p k t -> p (k t)"), bank[2][:, :], ACT.Copy)\
                        .then_inc(S["cb_kept"], 1)
                if gd:
                    z_keep(gd)
                if d == 0 and g >= 2:
                    group_squares(g - 2)
            group_squares(GROUPS - 2)
            group_roots(0, GROUPS - 1)
            for u in range(2):
                g_rounded(u)
            group_squares(GROUPS - 1)
            group_roots(GROUPS - 1, GROUPS)
            for u in range(2, INNER // P // 2):
                g_rounded(u)
            for o in range(7):
                hi_at(G["ssd_out"] + o + 3)

            squares("lat_f1", x, after("ssd_out"))
            root("lat_f1")
            rounded("lat_f1", u_hi, shifted(0, 2, 0))
            ffn(2)
            squares("l1_f0", x, after("ffn2"))
            root("l1_f0")
            rounded("l1_f0", u_hi, shifted(1, 0, 0))
            ffn(3)

            squares("l1_pool", x, after("ffn3"))
            root("l1_pool")
            rounded("l1_pool", u_hi, shifted(1, 1, 0))
            hi_at(G["pool"] + 2)
            for g in range(len(WINDOWS)):
                if g < len(WINDOWS) - 1:
                    act.wait_ge(S["pool_first"], g + 1)
                else:
                    act.wait_ge(S["chunk_used"], G["pool"] + 1)
                nc.scalar.activation(pq[:, :, g, :], bank[4 + g][:, :].rearrange("p (t n) -> p t n", t=TT), ACT.Copy)\
                    .then_inc(S["pool_kept"], 1)
            squares("l1_f1", x, after("pool"))
            root("l1_f1", 4)
            rounded("l1_f1", u_hi, shifted(1, 2, 0))
            ffn(4)
            squares("final", x, after("ffn4"))
            root("final")

            def pairs_of(t, n=256):
                return t[:, 0:TT * n].rearrange("p (t n) -> p t n", t=TT)

            act.wait_ge(S["lb_diff"], 1)
            nc.scalar.activation(small[:, 48:64], small[:, 48:64], ACT.Exp).then_inc(S["lb_exp"], 1)
            for l in range(DEPTH):
                squares(f"pre{l}", x, after("final" if l == 0 else "out0"))
                root(f"pre{l}")
                rounded(f"pre{l}", u_hi, lambda k: zero_col[:, 0:1])
                c0 = G[f"proj{l}"]
                hi_at(c0 + 2)
                dst = ([(hk[:, 2 * i:2 * i + 2, :], ACT.Copy) for i in range(4)]
                       + [(hq[:, 2 * i:2 * i + 2, :], ACT.Copy) for i in range(4)]
                       + [(hv[:, :, 256 * i:256 * i + 256], ACT.Copy) for i in range(4)]
                       + [(kvc[:, i, :, :], ACT.Copy) for i in range(2)] + [(ksw[:, i, :, :], ACT.Copy) for i in range(2)]
                       + [(vsw[:, i, :, :], ACT.Copy) for i in range(2)]
                       + [(nq[:, 2 * i:2 * i + 2, :], ACT.Copy) for i in range(4)] + [(gates[:, :, :], ACT.Sigmoid)]
                       + [(szh[:, 2 * i:2 * i + 2, :], ACT.Silu) for i in range(4)]
                       + [(snz[:, 2 * i:2 * i + 2, :], ACT.Silu) for i in range(4)])
                for i, (into, fn) in enumerate(dst):
                    act.wait_ge(S["chunk_used"], c0 + i + 1)
                    nc.scalar.activation(into, pairs_of(bank[4 + i % 3], PROJ[i][1]), fn).then_inc(S["proj_kept"], 1)
                    hi_at(c0 + i + 3)
                    if i == 4:
                        act.wait_ge(S["hgrn_step_v"], 3 * l + 1)
                        nc.scalar.activation(scratch[:, :, :], scratch[:, :, :], ACT.Exp).then_inc(S["hgrn_step_a"], 1)
                        act.wait_ge(S["hgrn_step_a"], 3 * l + 1)
                        nc.scalar.activation(qk[:, :, :], scratch[:, :, :], ACT.Ln, bias=1.0)\
                            .then_inc(S["hgrn_step_a"], 1)
                    if i == 5:
                        act.wait_ge(S["hgrn_step_v"], 3 * l + 3)
                        nc.scalar.activation(hk[:, :, :], hk[:, :, :], ACT.Exp).then_inc(S["hgrn_step_a"], 1)
                        if l:
                            nc.scalar.activation(qk[:, :, :], scratch[:, :, :], ACT.Exp).then_inc(S["hgrn_step_a"], 1)
                    if i == 6 and l:
                        act.wait_ge(S["hgrn_step_v"], 3 * l + 4)
                        nc.scalar.activation(scratch[:, :, :], qk[:, :, :], ACT.Ln).then_inc(S["hgrn_step_a"], 1)
                    for lev in range(NL):
                        if i == LEVEL_AT(lev) - 2:
                            buf = (qk, scratch)[lev % 2]
                            act.wait_ge(S["lev_diff"], 2 * (NL * l + lev + 1))
                            nc.scalar.activation(buf[:, :, :], buf[:, :, :], ACT.Exp).then_inc(S["lev_exp"], 1)
                    if i == LEVEL_AT(0):
                        act.wait_ge(S["lev_done"], (NL + 1) * l + 2)
                        for b in range(2):
                            nc.scalar.activation(attn_off[:, 4 * b:4 * b + 4, :].rearrange("p h t -> p (h t)"),
                                                 bank[b][:, :], ACT.Copy).then_inc(S["off_kept"], 1)
                    if i == AV_AT:
                        for b in range(4):
                            act.wait_ge(S["av_done"], 4 * l + b + 1)
                            nc.scalar.activation(o_h[:, 2 * b:2 * b + 2, :].rearrange("p h t -> p (h t)"),
                                                 bank[b][:, :], ACT.Copy).then_inc(S["o_kept"], 1)
                            nc.scalar.activation(scratch[:, 2 * b:2 * b + 2, :].rearrange("p h t -> p (h t)"),
                                                 bank[b][:, :], ACT.Square).then_inc(S["o_sq"], 1)
                    if i == AV_AT + 1:
                        act.wait_ge(S["o_stat"], l + 1)
                        nc.scalar.activation(small[:, 16:32], bank[7][:, 0:16], ACT.Sqrt, bias=EPS, scale=1.0 / P)\
                            .then_inc(S["o_root"], 1)
                    if i >= AV_AT + 2:
                        kv = i - AV_AT - 2
                        act.wait_ge(S["win_made"], 6 * l + 3 * kv + 3)
                        nc.scalar.activation(win_hi[kv][:, :, :, :], win[kv][:, :, :, :], ACT.Copy)\
                            .then_inc(S["win_hi_done"], 1)
                def score_exps(br, s):
                    nb = 2 * l + br
                    if br and s in (0, 2):
                        act.wait_ge(S["p_turned"], 6 * (nb - 1) + (2, 0, 6)[s])
                    act.wait_ge(S["score_max"], 6 * nb + s + 1)
                    heads = range(4 * s, 4 * s + 4) if s < 2 else range(2 * (s - 2), 2 * (s - 2) + 2)
                    n = P if s < 2 else T
                    for hh, h in enumerate(heads):
                        at = h if s < 2 else H2 + h
                        m = nc.scalar.activation((pr0 if s < 2 else pr1)[:, h, :], bank[s % 2][:, hh * n:(hh + 1) * n],
                                                 ACT.Exp, bias=sums[:, at:at + 1], scale=SCALE,
                                                 accum_out=sums[:, 16 + at:17 + at])
                    m.then_inc(S["score_exp"], 1)

                def keep_turned(br, n):
                    nb = 2 * l + br
                    act.wait_ge(S["p_turned"], 6 * nb + n + 1)
                    if n == 0 and br:
                        act.wait_ge(S["av2_done"], 4 * nb)
                    part, half = TURNS[n]
                    h0 = 4 * half
                    into = (pt0[:, h0:h0 + 4, 0:P], pt0[:, h0:h0 + 4, P:T], pt1[:, h0:h0 + 4, :])[part]
                    nc.scalar.activation(into, bank[2][:, :].rearrange("p (h t) -> p h t", h=4), ACT.Copy)\
                        .then_inc(S["p_kept_a"], 1)

                def hidden_silu(kv):
                    act.wait_ge(S["chunk_used"], c0 + 33 + 2 * kv)
                    if kv:
                        act.wait_ge(S["cmp_out"], 2 * l + 1)
                    nc.scalar.activation(hid[:, :, :].rearrange("p g n -> p (g n)"), bank[5 + kv][:, 0:32], ACT.Silu,
                                         bias=col("b1_v" if kv else "b1_k")[:, l:l + 1]).then_inc(S["cmp_silu"], 1)

                hi_at(c0 + 34)
                hi_at(c0 + 35)
                hidden_silu(0)
                score_exps(0, 0)
                score_exps(0, 1)
                act.wait_ge(S["cmp_out"], 2 * l + 1)
                nc.scalar.activation(kcmp[:, :, :].rearrange("p g n -> p (g n)"), bank[7][:, 0:32], ACT.Copy)\
                    .then_inc(S["cmp_kept"], 1)
                hi_at(c0 + 36)
                score_exps(0, 2)
                score_exps(0, 3)
                hidden_silu(1)
                hi_at(c0 + 37)
                score_exps(0, 4)
                score_exps(0, 5)
                act.wait_ge(S["cmp_out"], 2 * l + 2)
                nc.scalar.activation(vcmp[0:16, :, :].rearrange("p g n -> p (g n)"), bank[5][0:16, 0:256], ACT.Copy)\
                    .then_inc(S["cmp_kept"], 1)
                act.wait_ge(S["c_diff"], l + 1)
                nc.scalar.activation(prc[:, :, :, :], prc[:, :, :, :], ACT.Exp, scale=SCALE).then_inc(S["c_exp"], 1)
                keep_turned(0, 0)
                score_exps(1, 0)
                score_exps(1, 1)
                for hp in range(4):
                    act.wait_ge(S["c_turned"], 4 * l + hp + 1)
                    nc.scalar.activation(ptc[0:16, 2 * hp:2 * hp + 2, :].rearrange("p h t -> p (h t)"),
                                         bank[2 + hp % 2][0:16, :], ACT.Copy).then_inc(S["c_kept"], 1)
                keep_turned(0, 2)
                keep_turned(0, 4)
                for b in range(4):
                    act.wait_ge(S["o_gated"], 4 * l + b + 1)
                    nc.scalar.activation(fin_hi[:, 2 * b:2 * b + 2, :], scratch[:, 2 * b:2 * b + 2, :], ACT.Copy)\
                        .then_inc(S["fin_hi_done"], 1)
                for s in range(2, 6):
                    score_exps(1, s)
                for n in (0, 2, 4):
                    keep_turned(1, n)
                for hp in range(4):
                    act.wait_ge(S["n_gated"], 4 * l + hp + 1)
                    nc.scalar.activation(fin_hi[:, H2 + 2 * hp:H2 + 2 * hp + 2, :], scratch[:, 2 * hp:2 * hp + 2, :],
                                         ACT.Copy).then_inc(S["fin_hi_done"], 1)
                for o in range(4):
                    for kh in range(2):
                        i = 35 + 2 * o + kh
                        if kh:
                            act.wait_ge(S["chunk_used"], c0 + i + 1)
                            nc.scalar.activation(y_out[:, 2 * o:2 * o + 2, :].rearrange("p k t -> p (k t)"),
                                                 bank[o % 3][:, :], ACT.Copy).then_inc(S["out_kept"], 1)
                            for blk in range(2):
                                nc.scalar.activation(scratch[:, 2 * o + blk, :], bank[o % 3][:, blk * T:(blk + 1) * T],
                                                     ACT.Square).then_inc(S["squares"], 1)
                        if i < 42:
                            hi_at(c0 + i + 3)
                root(f"post{l}")
            for n in (0, 2):
                act.wait_ge(S["x_out_turned"], n + 1)
                nc.scalar.activation(x_out[:, n // 2, 0:512], bank[4 + n][:, :], ACT.Copy).then_inc(S["x_out_kept"], 1)

        @block.vector
        def _(ve):
            steps = [0]

            def step():
                steps[0] += 1
                return steps[0]

            def lo(c, n=CH, j=0):
                slot = c % SLOTS
                ve.wait_ge(S["hi_done"], c + 1 + SLOTS * j)
                ve.tensor_tensor(wlo[slot][:, 0:n], raw[slot][:, 0:n], whi[slot][:, 0:n].bitcast(F32), ALU.subtract)\
                    .then_inc(lo_done[slot], 1)

            def lo_at(c):
                if c < CHUNKS:
                    lo(c, CHUNK_FLOATS.get(c, CH))

            def recip(name):
                n = N[name]
                ve.wait_ge(S["root_done"], n + 1)
                ve.reciprocal(rstd[n % 2][:, :], rms[n % 2][:, :]).then_inc(S["recip_done"], 1)

            def modulation(l, s, v):
                ve.wait_ge(S["mods_done"], ADA_CHUNKS * l + 4 * (3 * s + 2))
                at = 8 * (3 * s + 1)
                g0 = 8 * (3 * l + s)
                ve.scalar_tensor_tensor(mod_a[:, :], mods[l][:, at:at + 8, v], 1.0, col("norm_g")[:, g0:g0 + 8],
                                        ALU.add, ALU.mult).then_inc(S["dve_step"], 1)
                ve.wait_ge(S["dve_step"], step())

            def apply(name, src, scale, shift, dst_hi, dst_lo):
                ve.wait_ge(S["recip_done"], N[name] + 1)
                for k in range(KB + 1):
                    if k < KB:
                        ve.scalar_tensor_tensor(scratch[:, k, :], src[:, k, :], scale[:, k:k + 1],
                                                rstd[N[name] % 2][:, :], ALU.mult, ALU.mult).then_inc(S["scaled"], 1)
                    if k:
                        b = k - 1
                        ve.wait_ge(S["u_hi_done"], 8 * NSP[name] + k)
                        ve.scalar_tensor_tensor(dst_lo[:, b, :], scratch[:, b, :], shift(b),
                                                dst_hi[:, b, :].bitcast(F32), ALU.add, ALU.subtract)\
                            .then_inc(S["u_done"], 1)

            def shifted(l, s, v):
                return lambda k: mods[l][:, 8 * 3 * s + k, v:v + 1]

            def ada_sum(q, slot, loads, buf, vectors, before):
                ve.wait_ge(ada_in[slot], 16 * loads)
                for k in range(KB):
                    for v in range(vectors):
                        acc, w, c = ada_acc[buf][:, v, :], ada[slot][:, k, :], scv[:, k, v:v + 1]
                        if k:
                            ve.wait_ge(S["ada_step"], before + vectors * (k - 1) + v + 1)
                            m = ve.scalar_tensor_tensor(acc, w, c, acc, ALU.mult, ALU.add)
                        else:
                            m = ve.tensor_scalar(acc, w, c, None, ALU.mult)
                        if k < KB - 1:
                            m.then_inc(S["ada_step"], 1)
                m.then_inc(S["ada_acc"], 1)

            def ada_keep(q, vectors):
                ve.wait_ge(S["ada_done"], q + 2)
                ve.tensor_tensor(mods_all[:, bass.ds(2 * q, 4), 0:vectors],
                                 bank[2][:, 0:8].rearrange("p (b v) -> p b v", v=2)[:, :, 0:vectors],
                                 cols[:, bass.ds(2 * q, 4)].unsqueeze(2).to_broadcast([P, 4, vectors]), ALU.add)\
                    .then_inc(S["mods_done"], 2)

            def ffn(i, beside=None):
                name, l, s = FFNS[i]
                g = G[name]
                dst, v = (xc, 1) if i == 0 else (x, 0)
                q0 = ADA_FIRST + ADA_FFN * i
                pairs = FP * i

                def mult(j):
                    ve.wait_ge(S["silu_done"], pairs + j)
                    ve.wait_ge(S["chunk_used"], g + 3 * j - 1)
                    ve.tensor_tensor(hf[:, :], hs[:, :], bank[1][:, :], ALU.mult).then_inc(S["mult_done"], 1)
                    ve.wait_ge(S["h_hi_done"], pairs + j)
                    ve.tensor_tensor(h_lo[:, :, :].rearrange("p k t -> p (k t)"), hf[:, :],
                                     h_hi[:, :, :].rearrange("p k t -> p (k t)").bitcast(F32), ALU.subtract)\
                        .then_inc(S["h_done"], 1)

                def sum_of(q, n, half_q, vectors):
                    if vectors == 2:
                        before = (KB - 1) * 2 * (ADA_FIRST // 2 + q - ADA_FIRST)
                    else:
                        before = (KB - 1) * (2 * (ADA_BOTH - ADA_FIRST // 2) + q - ADA_BOTH)
                    ada_sum(q, n, half_q - ADA_FIRST // 2 + 2, n, vectors, before)

                lo_at(g + 2)
                if beside:
                    beside()

                def pair(j, q, half_q, last, vectors):
                    mult(j)
                    if i not in UPS_BY_POOL:
                        lo(g + 4, CH, j - 1)
                    if vectors:
                        sum_of(q, 0, half_q, vectors)
                    if not last and i not in GATES_BY_POOL:
                        lo(g + 5, CH, j - 1)
                    if vectors:
                        sum_of(q + 1, 1, half_q, vectors)
                        ada_keep(q, vectors)

                for j0, j1, vectors in ADA_PAIRS[i]:
                    with ve.Fori(j0, min(j1, FP - 1)) as j:
                        pair(j, q0 + 2 * (j - 1), q0 // 2 + (j - 1), False, vectors)
                pair(FP - 1, q0 + 2 * (FP - 2), q0 // 2 + FP - 2, True, vectors)
                lo_at(g + 3 * FP - 1)
                mult(FP)
                lo_at(g + 3 * FP)
                lo_at(g + 3 * FP + 1)
                ve.wait_ge(S["mods_done"], ADA_CHUNKS * l + 4 * (6 * s + 3))
                at = 8 * (6 * s + 2)
                ve.tensor_scalar(gate[:, :], mods[l][:, at:at + 8, v], 0.5, None, ALU.mult).then_inc(S["dve_step"], 1)
                ve.wait_ge(S["dve_step"], step())
                for b in range(KB):
                    if b < 6:
                        ve.wait_ge(S["y_done"], 3 * i + b // 2 + 1)
                    else:
                        ve.wait_ge(S["chunk_used"], g + 3 * FP)
                    ve.scalar_tensor_tensor(dst[:, b, :], bank[4 + b // 2][:, (b % 2) * T:(b % 2 + 1) * T],
                                            gate[:, b:b + 1], dst[:, b, :], ALU.mult, ALU.add)\
                        .then_inc(S["x_done"], 1)

            ve.wait_ge(S["set_up"], 3)
            ve.wait_ge(S["cols_turned"], ROW_TILES)
            ve.tensor_copy(cols[:, 0:4 * P], bank[0][:, :]).then_inc(S["cols_done"], 1)
            ve.tensor_copy(cols[:, 4 * P:4 * P + LAST_ROWS], bank[1][:, 0:LAST_ROWS]).then_inc(S["cols_done"], 1)
            for n in range(8):
                ve.wait_ge(S["x_turned"], n + 1)
                pr = n % 4
                ve.tensor_copy((xc, x)[n // 4][:, 2 * pr:2 * pr + 2, :].rearrange("p k t -> p (k t)"),
                               bank[4 + pr][:, :]).then_inc(S["x_done"], 1)
            ve.wait_ge(S["cols_done"], 2)
            for n in range(ADA_FIRST // 2):
                q = 2 * n + 1
                if n == 0:
                    ve.wait_ge(S["silu_c"], 2)
                if n >= 2:
                    ve.wait_ge(S["ada_done"], 2 * n - 1)
                ada_sum(q, q, 1, n % 2, 2, 2 * (KB - 1) * n)
                if n == 1:
                    recip("ctx_f0")
                    recip("lat_f0")
            lo_at(0)
            lo_at(1)
            ve.wait_ge(S["ada_done"], ADA_FIRST)
            ve.tensor_tensor(mods_all[:, 0:2 * ADA_FIRST, :],
                             bank[2][:, 0:4 * ADA_FIRST].rearrange("p (b v) -> p b v", v=2),
                             cols[:, 0:2 * ADA_FIRST].unsqueeze(2).to_broadcast([P, 2 * ADA_FIRST, 2]), ALU.add)\
                .then_inc(S["mods_done"], ADA_FIRST)
            modulation(0, 0, 1)
            apply("ctx_f0", xc, mod_a, shifted(0, 0, 1), uc_hi, uc_lo)
            modulation(0, 0, 0)
            apply("lat_f0", x, mod_a, shifted(0, 0, 0), u_hi, u_lo)
            ve.wait_ge(S["mask_in"], 16)
            ve.tensor_copy(level_mask[:, :, :], mask_in[:, :, :]).then_inc(S["dve_step"], 1)
            step()
            ffn(0)

            def ctx_norm():
                recip("ctx_ssd")
                modulation(0, 1, 1)
                apply("ctx_ssd", xc, mod_a, shifted(0, 1, 1), uc_hi, uc_lo)

            ffn(1, ctx_norm)

            modulation(0, 1, 0)
            recip("lat_ssd")
            apply("lat_ssd", x, mod_a, shifted(0, 1, 0), u_hi, u_lo)
            c0 = G["ssd_in"]
            lo_at(c0 + 2)
            R, RF, RB = slice(64, P), slice(64, 96), slice(96, P)
            v_, t1, e_, t3, z_, z2, pl = [t[R, :] for t in dtt]
            ve.wait_ge(S["chunk_used"], c0 + 1)
            ve.wait_ge(S["ssd_in"], 48)
            ve.tensor_scalar(v_, bank[2][R, :], acol[R, 1:2], None, ALU.add).then_inc(S["dt_taken"], 1)
            ve.wait_ge(S["dt_taken"], 1)
            ve.scalar_tensor_tensor(t1, v_, -1.0, v_, ALU.mult, ALU.min).then_inc(S["dt_taken"], 1)
            ve.wait_ge(S["dt_exp"], 2)
            ve.tensor_scalar(t3, e_, 2.0, None, ALU.add).then_inc(S["dve_step"], 1)
            ve.wait_ge(S["dve_step"], step())
            ve.reciprocal(t3, t3).then_inc(S["dve_step"], 1)
            ve.wait_ge(S["dve_step"], step())
            ve.tensor_tensor(z_, e_, t3, ALU.mult).then_inc(S["dve_step"], 1)
            ve.wait_ge(S["dve_step"], step())
            ve.tensor_tensor(z2, z_, z_, ALU.mult).then_inc(S["dve_step"], 1)
            ve.wait_ge(S["dve_step"], step())
            ve.tensor_scalar(pl, z2, 1.0 / 15, None, ALU.mult).then_inc(S["dve_step"], 1)
            for odd in (13, 11, 9, 7, 5, 3):
                ve.wait_ge(S["dve_step"], step())
                ve.scalar_tensor_tensor(pl, pl, 1.0 / odd, z2, ALU.add, ALU.mult).then_inc(S["dve_step"], 1)
            ve.wait_ge(S["dve_step"], step())
            ve.scalar_tensor_tensor(pl, pl, 1.0, z_, ALU.add, ALU.mult).then_inc(S["dve_step"], 1)
            ve.tensor_scalar(t1, v_, 0.0, None, ALU.max).then_inc(S["dve_step"], 1)
            step()
            ve.wait_ge(S["dve_step"], step())
            dt = v_
            ve.scalar_tensor_tensor(dt, pl, 2.0, t1, ALU.mult, ALU.add).then_inc(S["dve_step"], 1)
            ve.wait_ge(S["dve_step"], step())
            ve.tensor_scalar(t1, dt, acol[R, 2:3], -1.0, ALU.mult, ALU.mult).then_inc(S["dve_step"], 1)
            ve.wait_ge(S["dve_step"], step())
            for s in range(2):
                ve.tensor_tensor_scan(t3[:, s * T:(s + 1) * T], ones[R, 0:1].to_broadcast([64, T]),
                                      t1[:, s * T:(s + 1) * T], 0.0, ALU.mult, ALU.add).then_inc(S["dve_step"], 1)
                step()
            ve.wait_ge(S["dve_step"], steps[0])
            sum_f, sum_b = dtt[3][RF, :], dtt[3][RB, :]
            ve.tensor_copy(q_rows[RF, :], sum_f[:, 0:T]).then_inc(S["dve_step"], 1)
            ve.memset(acol[RF, 3:4], 0.0).then_inc(S["dve_step"], 1)
            ve.tensor_copy(acol[RB, 3:4], sum_b[:, T - 1:T]).then_inc(S["dve_step"], 1)
            for n in range(3):
                step()
            ve.wait_ge(S["dve_step"], steps[0])
            ve.tensor_tensor(q_rows[RB, :], dtt[1][RB, 0:T], sum_b[:, 0:T], ALU.subtract).then_inc(S["dt_cols"], 2)
            ve.tensor_scalar(dtt[4][RF, 0:T], sum_f[:, T:2 * T], -1.0, sum_f[:, 2 * T - 1:2 * T], ALU.mult, ALU.add)\
                .then_inc(S["dve_step"], 1)
            ve.wait_ge(S["dve_step"], step())
            ve.tensor_tensor(dtt[4][RB, 0:T], sum_b[:, T:2 * T], dtt[1][RB, T:2 * T], ALU.subtract)\
                .then_inc(S["dt_cols"], 1)
            ve.wait_ge(S["dt_exp"], 4)
            ve.tensor_tensor(pl[:, 0:T], e_[:, 0:T], dt[:, T:2 * T], ALU.mult).then_inc(S["dt_cols"], 1)

            def ctx_keep(i):
                xi = i - 4
                src = bank[2][:, :].rearrange("p (t n) -> p t n", t=TT)
                if i < 2:
                    ve.wait_ge(S["turned"], i + 1)
                    ve.tensor_copy(Bc_tok[:, :, 256 * i:256 * i + 256], src).then_inc(S["ctx_kept"], 1)
                else:
                    g = xi // 2
                    ve.wait_ge(S["turned"], 4 + 2 * xi)
                    ve.wait_ge(S["tok_done"], 1)
                    if g >= 2:
                        ve.wait_ge(S["state_done"], 2 * (g - 1))
                    for d in range(2):
                        for tile in range(TT):
                            h0 = d * HEADS + 4 * xi
                            w = tokc[:, 3, tile, h0:h0 + 4].unsqueeze(2).to_broadcast([P, 4, HP])
                            m = ve.tensor_tensor(
                                xw[g % 2][:, d, tile, (xi % 2) * 256:(xi % 2) * 256 + 256]
                                .rearrange("p (h q) -> p h q", q=HP),
                                src[:, tile, :].rearrange("p (h q) -> p h q", q=HP), w, ALU.mult)
                        m.then_inc(S["ctx_kept"], 1)

            def conv(i):
                ns = 1 if i in (2, 3) else 2
                m0 = (SSD_COLS[i] - INNER) // P
                ve.wait_ge(S["conv_in"], CONV_IN[i])
                if i:
                    ve.wait_ge(S["conv_silu"], CONV_SILU[i - 1])
                for w in range(CONV_W):
                    if w:
                        ve.wait_ge(S["dve_step"], steps[0])
                    for blk in range(2):
                        acc = cacc[:, blk, 0:ns, :]
                        src = cpad[i % 2][:, blk, 0:ns, w:w + T]
                        wc = col("conv_w")[:, 24 * w + m0 + blk:24 * w + m0 + blk + 1]
                        if w == 0:
                            m = ve.tensor_scalar(acc, src, wc, col("conv_b")[:, m0 + blk:m0 + blk + 1],
                                                 ALU.mult, ALU.add)
                        else:
                            m = ve.scalar_tensor_tensor(acc, src, wc, acc, ALU.mult, ALU.add)
                        if w < CONV_W - 1:
                            m.then_inc(S["dve_step"], 1)
                            step()
                m.then_inc(S["conv_done"], 1)

            for i in range(12):
                conv(i)
                if i in (1, 2) or i >= 5:
                    ctx_keep(i - 1)
                if i == 3:
                    ve.wait_ge(S["tok_turned"], 1)
                    ve.tensor_copy(tokc[:, :, :, :].rearrange("p w t c -> p (w t c)"), bank[3][:, :])\
                        .then_inc(S["tok_done"], 1)
            ctx_keep(11)
            lo_at(c0 + 16)
            n = 0
            for tile in range(TT):
                for g in range(GROUPS):
                    ve.wait_ge(S["skip_done"], (1 + (g == 3), 3 + g // 2)[tile])
                    for d in range(2):
                        h0 = d * HEADS + g * EH
                        yg = y[:, tile, 512 * g:512 * g + 512]
                        ve.wait_ge(S["off_done"], n + 1)
                        ve.tensor_tensor(tmp_off[:, n % 2, :].rearrange("p (h q) -> p h q", q=HP),
                                         bank[n % 4][:, :].rearrange("p (h q) -> p h q", q=HP),
                                         tokc[:, 2, tile, h0:h0 + EH].unsqueeze(2).to_broadcast([P, EH, HP]),
                                         ALU.mult).then_inc(S["off_added"], 1)
                        n += 1
                        ve.wait_ge(S["off_added"], n)
                        if d:
                            ve.wait_ge(S["dve_step"], steps[0])
                        ve.tensor_tensor(yg, yg, tmp_off[:, (n - 1) % 2, :], ALU.add).then_inc(S["dve_step"], 1)
                        step()

            def seg(gd):
                g, d = gd // 2, gd % 2
                if gd >= 2:
                    ve.wait_ge(S["diag_done"], gd - 1)
                if gd == 1:
                    ve.wait_ge(S["seg_done"], 2)
                for h in range(EH):
                    if h % (EH // 2) == 0:
                        part = h // (EH // 2)
                        ve.wait_ge(q_loaded[part] if gd else q_first_loaded[part], 16 * max(gd, 1))
                    at = d * HEADS + g * EH + h
                    q_of = qb[:, h, :] if gd else q_first[h // (EH // 2)][:, h % (EH // 2), :]
                    ve.scalar_tensor_tensor(e_long[d][:, h, :], q_of, tokc[:, 0, d, at:at + 1],
                                            mask_b if d else mask_f, ALU.subtract, ALU.min)
                    own = slice(P * (1 - d), P * (2 - d))
                    m = ve.scalar_tensor_tensor(e_short[d][:, h, :], q_of[:, own], tokc[:, 0, 1 - d, at:at + 1],
                                                mask_b[:, P:T] if d else mask_f[:, 0:P], ALU.subtract, ALU.min)
                    if h % (EH // 2) == EH // 2 - 1:
                        m.then_inc(S["seg_done"], 1)

            def decay(gd):
                g, d = gd // 2, gd % 2
                own = slice(P * (1 - d), P * (2 - d))
                ve.wait_ge(S["cb_kept"], g + 1)
                for h in range(EH):
                    part = h // (EH // 2)
                    if h % (EH // 2) == 0:
                        ve.wait_ge(S["e_done"], 2 * gd + part + 1)
                    at = d * HEADS + g * EH + h
                    ve.scalar_tensor_tensor(e_long[d][:, h, :], e_long[d][:, h, :], tokc[:, 1, d, at:at + 1],
                                            cb[:, d, :], ALU.mult, ALU.mult)
                    m = ve.scalar_tensor_tensor(e_short[d][:, h, :], e_short[d][:, h, :],
                                                tokc[:, 1, 1 - d, at:at + 1], cb[:, 1 - d, own], ALU.mult, ALU.mult)
                    if h % (EH // 2) == EH // 2 - 1:
                        m.then_inc(S["m_done"], 1)

            def add_diag(g):
                ve.wait_ge(S["diag_done"], 2 * g + 2)
                ve.wait_ge(S["z_kept"], 2 * g + 2)
                for tile in range(TT):
                    yg = y[:, tile, 512 * g:512 * g + 512]
                    ve.tensor_tensor(yg, yg, bank[DIAG_BANKS[g % 2][tile]][:, :], ALU.add).then_inc(S["y_added"], 1)
                    ve.wait_ge(S["y_added"], 2 * g + tile + 1)
                    ve.tensor_tensor(yg, yg, sz[:, tile, 512 * g:512 * g + 512], ALU.mult).then_inc(S["gated"], 1)

            ve.wait_ge(S["dve_step"], steps[0])
            for gd in range(2 * GROUPS):
                seg(gd)
                if gd in (3, 5):
                    add_diag(gd // 2 - 1)
                decay(gd)
            add_diag(GROUPS - 2)
            lo_at(c0 + 23)

            def group_norm(g0, g1):
                ve.wait_ge(S["g_root"], 1 if g0 == 0 else 2)
                ve.reciprocal(small[:, 16 + 2 * g0:16 + 2 * g1], small[:, 24 + 2 * g0:24 + 2 * g1])\
                    .then_inc(S["dve_step"], 1)
                ve.wait_ge(S["dve_step"], step())
                for g in range(g0, g1):
                    for tile in range(TT):
                        yg = y[:, tile, 512 * g:512 * g + 512]
                        at = 16 + 2 * g + tile
                        ve.tensor_scalar(yg, yg, small[:, at:at + 1], None, ALU.mult).then_inc(S["g_norm"], 1)

            def g_rest(k):
                ve.wait_ge(S["g_hi_kept"], k // 2 * 2 + 2)
                ve.scalar_tensor_tensor(g_lo[:, k, :], bank[G_BANKS[k // 2 % 4]][:, (k % 2) * T:(k % 2 + 1) * T],
                                        col("ssd_norm")[:, k:k + 1], g_hi[:, k, :].bitcast(F32),
                                        ALU.mult, ALU.subtract).then_inc(S["g_ready"], 1)

            group_norm(0, GROUPS - 1)
            add_diag(GROUPS - 1)
            for k in range(4):
                g_rest(k)
            group_norm(GROUPS - 1, GROUPS)
            for k in range(4, INNER // P):
                g_rest(k)
            for o in range(4):
                for kh in range(2):
                    if kh:
                        ve.wait_ge(S["chunk_used"], G["ssd_out"] + 2 * o + 2)
                        for blk in range(2):
                            b = 2 * o + blk
                            ve.scalar_tensor_tensor(x[:, b, :], bank[5 + o % 3][:, blk * T:(blk + 1) * T],
                                                    mods[0][:, 8 * 5 + b, 0:1], x[:, b, :], ALU.mult, ALU.add)\
                                .then_inc(S["x_done"], 1)
                    if 2 * o + kh < 7:
                        lo_at(G["ssd_out"] + 2 * o + kh + 3)

            modulation(0, 2, 0)
            recip("lat_f1")
            apply("lat_f1", x, mod_a, shifted(0, 2, 0), u_hi, u_lo)
            ffn(2)
            modulation(1, 0, 0)
            recip("l1_f0")
            apply("l1_f0", x, mod_a, shifted(1, 0, 0), u_hi, u_lo)
            ffn(3)

            modulation(1, 1, 0)
            recip("l1_pool")
            apply("l1_pool", x, mod_a, shifted(1, 1, 0), u_hi, u_lo)
            lo_at(G["pool"] + 2)
            ve.tensor_tensor(ps_cols[:, 0, :], col("pool_scale"), mods[1][:, 40:48, 0], ALU.mult)\
                .then_inc(S["dve_step"], 1)
            ve.wait_ge(S["dve_step"], step())
            ve.tensor_tensor(ps_cols[:, 1, :], col("pool_b"), ps_cols[:, 0, :], ALU.mult).then_inc(S["dve_step"], 1)
            ve.wait_ge(S["dve_step"], step())
            for b in range(KB):
                ve.wait_ge(S["pool_done"], b // 2 + 1)
                ve.tensor_scalar(scratch[:, b, :], bank[b // 2][:, (b % 2) * T:(b % 2 + 1) * T], ps_cols[:, 0, b:b + 1],
                                 ps_cols[:, 1, b:b + 1], ALU.mult, ALU.add).then_inc(S["dve_step"], 1)
                ve.wait_ge(S["dve_step"], step())
                ve.tensor_tensor(x[:, b, :], x[:, b, :], scratch[:, b, :], ALU.add).then_inc(S["x_done"], 1)
            modulation(1, 2, 0)
            recip("l1_f1")
            apply("l1_f1", x, mod_a, shifted(1, 2, 0), u_hi, u_lo)
            ffn(4)
            recip("final")
            ve.wait_ge(S["recip_done"], N["final"] + 1)
            for k in range(KB):
                ve.scalar_tensor_tensor(x[:, k, :], x[:, k, :], col("final_g")[:, k:k + 1], rstd[N["final"] % 2][:, :],
                                        ALU.mult, ALU.mult).then_inc(S["x_done"], 1)

            def softmax_scale(l, total, w, gate_):
                ve.tensor_scalar(w, total, 1e-30, None, ALU.max).then_inc(S["dve_step"], 1)
                ve.wait_ge(S["dve_step"], step())
                ve.reciprocal(w, w).then_inc(S["dve_step"], 1)
                ve.wait_ge(S["dve_step"], step())
                ve.wait_ge(S["proj_kept"], NP_ * l + 23)
                ve.tensor_tensor(w, w, gate_, ALU.mult).then_inc(S["dve_step"], 1)
                ve.wait_ge(S["dve_step"], step())

            def gate_cols(branch):
                return gates[:, :, :].rearrange("p t (h b) -> p t h b", b=3)[:, :, :, branch]

            def rope(t, sin, cos, ps, shape):
                tmp = rtmp[:, 0:shape[1], 0:shape[2]]
                ve.tensor_tensor(tmp, ps, sin.unsqueeze(1).to_broadcast(shape), ALU.mult).then_inc(S["dve_step"], 1)
                ve.tensor_tensor(t, t, cos.unsqueeze(1).to_broadcast(shape), ALU.mult).then_inc(S["dve_step"], 1)
                step()
                ve.wait_ge(S["dve_step"], step())
                return ve.tensor_tensor(t, t, tmp, ALU.add)

            def keep_level(l, i):
                ve.wait_ge(S["lev_done"], (NL + 1) * l + i + 2)
                if i < 0:
                    ve.wait_ge(S["attn_zero"], l + 1)
                flat = attn[:, :, :, :].rearrange("p h t q -> p (h t) q")
                which = NL - 1 if i < 0 else i - 1
                for b in range(4):
                    ve.copy_predicated(flat[:, 4 * b:4 * b + 4, :],
                                       level_mask[:, which, :].unsqueeze(1).to_broadcast([P, 4, P]),
                                       bank[b][:, :].rearrange("p (u q) -> p u q", u=4)).then_inc(S["lev_kept"], 1)

            lbc = sums[:, 48:64].rearrange("p (i h) -> p i h", h=H2)
            e2 = small[:, 48:64].rearrange("p (i h) -> p i h", h=H2)
            lg = col("lb").rearrange("p (i h) -> p i h", h=H2)
            ve.tensor_tensor(lbc[:, 0, :], lg[:, 0, :], lg[:, 1, :], ALU.max).then_inc(S["dve_step"], 1)
            ve.wait_ge(S["dve_step"], step())
            ve.tensor_tensor(e2, lg, lbc[:, 0, :].unsqueeze(1).to_broadcast([P, 2, H2]), ALU.subtract)\
                .then_inc(S["lb_diff"], 1)
            ve.wait_ge(S["lb_exp"], 1)
            ve.tensor_tensor(lbc[:, 0, :], e2[:, 0, :], e2[:, 1, :], ALU.add).then_inc(S["dve_step"], 1)
            ve.wait_ge(S["dve_step"], step())
            ve.reciprocal(lbc[:, 0, :], lbc[:, 0, :]).then_inc(S["dve_step"], 1)
            ve.wait_ge(S["dve_step"], step())
            ve.tensor_tensor(e2, e2, lbc[:, 0, :].unsqueeze(1).to_broadcast([P, 2, H2]), ALU.mult)\
                .then_inc(S["dve_step"], 1)
            ve.wait_ge(S["dve_step"], step())
            ve.tensor_tensor(lbc[:, 0, :], e2[:, 0, :], e2[:, 1, :], ALU.add).then_inc(S["dve_step"], 1)
            ve.wait_ge(S["dve_step"], step())
            ve.tensor_tensor(e2[:, 1, :], lbc[:, 0, :], e2[:, 0, :], ALU.subtract).then_inc(S["dve_step"], 1)
            ve.wait_ge(S["dve_step"], step())
            ve.tensor_scalar(e2[:, 1, :], e2[:, 1, :], 0.0, None, ALU.max).then_inc(S["dve_step"], 1)
            ve.wait_ge(S["dve_step"], step())
            ve.tensor_scalar(lbc[:, 0, :], e2[:, 1, :], 2.0 ** -64, None, ALU.max).then_inc(S["dve_step"], 1)
            ve.tensor_scalar(lbc[:, 1, :], e2[:, 1, :], -1.0, 1.0, ALU.mult, ALU.add).then_inc(S["dve_step"], 1)
            step()
            ve.wait_ge(S["dve_step"], step())
            for l in range(DEPTH):
                recip(f"pre{l}")
                apply(f"pre{l}", x, col("pre")[:, 8 * l:8 * l + 8], lambda k: zero_col[:, 0:1], u_hi, u_lo)
                c0 = G[f"proj{l}"]
                kept = NP_ * l
                va, aa = 3 * l, 3 * l
                lo_at(c0 + 2)
                for i in range(NP_):
                    if i == DIAG_AT + 1:
                        keep_level(l, -1)
                    for lev in range(1, NL):
                        if i == LEVEL_AT(lev) + 1:
                            keep_level(l, lev)
                    for lev in range(NL):
                        if i == LEVEL_AT(lev) - 1:
                            bv = halves((qk, scratch)[lev % 2], LEVELS[lev])
                            ve.wait_ge(S["lev_exp"], NL * l + lev + 1)
                            ve.wait_ge(S["proj_kept"], kept + 8)
                            ve.tensor_tensor(bv[:, :, 1, :], bv[:, :, 1, :], halves(hq, LEVELS[lev])[:, :, 1, :], ALU.mult)
                            ve.tensor_tensor(bv[:, :, 0, :], bv[:, :, 0, :], halves(hk, LEVELS[lev])[:, :, 0, :], ALU.mult)\
                                .then_inc(S["lev_ready"], 1)
                    if i == NP_ - 1:
                        ve.wait_ge(S["proj_kept"], kept + 27)
                        for b in range(4):
                            hs2 = slice(2 * b, 2 * b + 2)
                            ve.wait_ge(S["o_rstd"], 4 * l + b + 1)
                            ve.scalar_tensor_tensor(scratch[:, hs2, :], o_h[:, hs2, :], col("out_norm")[:, l:l + 1],
                                                    bank[b][:, :].rearrange("p (h t) -> p h t", h=2), ALU.mult, ALU.mult)\
                                .then_inc(S["dve_step"], 1)
                            step()
                        for b in range(4):
                            hs2 = slice(2 * b, 2 * b + 2)
                            ve.wait_ge(S["dve_step"], steps[0] - 3 + b)
                            ve.tensor_tensor(scratch[:, hs2, :], scratch[:, hs2, :], szh[:, hs2, :], ALU.mult)\
                                .then_inc(S["o_gated"], 1)
                    lo_at(c0 + i + 3)
                    if i == 4:
                        ve.wait_ge(S["proj_kept"], kept + 4)
                        ve.scalar_tensor_tensor(scratch[:, :, :], hk[:, :, :], -1.0, hk[:, :, :], ALU.mult, ALU.min)\
                            .then_inc(S["hgrn_step_v"], 1)
                    if i == 5:
                        ve.wait_ge(S["hgrn_step_a"], aa + 2)
                        ve.scalar_tensor_tensor(scratch[:, :, :], hk[:, :, :], 0.0, qk[:, :, :], ALU.min, ALU.subtract)\
                            .then_inc(S["hgrn_step_v"], 1)
                        ve.wait_ge(S["hgrn_step_v"], va + 2)
                        ve.tensor_tensor(hk[:, :, :], scratch[:, :, :], hk[:, :, :], ALU.subtract)\
                            .then_inc(S["hgrn_step_v"], 1)
                    if i == 6 and l:
                        ve.wait_ge(S["hgrn_step_a"], aa + 4)
                        for h in range(H2):
                            m = ve.tensor_scalar(qk[:, h, :], qk[:, h, :], lbc[:, 1, h:h + 1], lbc[:, 0, h:h + 1],
                                                 ALU.mult, ALU.add)
                        m.then_inc(S["hgrn_step_v"], 1)
                        for h in range(H2):
                            m = ve.tensor_scalar(hk[:, h, :], hk[:, h, :], lbc[:, 1, h:h + 1], None, ALU.mult)
                        m.then_inc(S["dve_step"], 1)
                        step()
                    if i == 7:
                        if l:
                            ve.wait_ge(S["hgrn_step_a"], aa + 5)
                        for h in range(H2):
                            m = ve.tensor_tensor_scan(hb[:, h, :], ones[:, 0:1].to_broadcast([P, T]), scratch[:, h, :],
                                                      0.0, ALU.mult, ALU.add)
                        m.then_inc(S["scan_done"], 1)
                    for r in range(6):
                        if i == ROPE_AT[r]:
                            ve.wait_ge(S["roped"], 6 * l + r + 1)
                            t = ksw[0:ROT, r, :, :] if r < 2 else nq[0:ROT, 2 * (r - 2):2 * (r - 2) + 2, :]
                            rope(t, sin_t, cos_t, bank[7][0:ROT, :].rearrange("p (g t) -> p g t", g=2), [ROT, 2, T])\
                                .then_inc(S["rope_done"], 1)
                    if i == AV_AT + 1:
                        ve.wait_ge(S["o_root"], l + 1)
                        ve.reciprocal(small[:, 32:48], small[:, 16:32]).then_inc(S["o_recip"], 1)
                    if i >= AV_AT + 2:
                        kv = i - AV_AT - 2
                        ve.wait_ge(S["win_hi_done"], 2 * l + kv + 1)
                        ve.tensor_tensor(win_lo[kv][:, :, :, :], win[kv][:, :, :, :], win_hi[kv][:, :, :, :].bitcast(F32),
                                         ALU.subtract).then_inc(S["win_done"], 1)

                def score_max(br, s):
                    ve.wait_ge(S["score_done"], 12 * l + 6 * br + s + 1)
                    nh = 4 if s < 2 else 2
                    at = 4 * s if s < 2 else H2 + 2 * (s - 2)
                    ve.tensor_reduce(sums[:, at:at + nh], bank[s % 2][:, :].rearrange("p (h s) -> p h s", h=nh),
                                     AX.X, ALU.max).then_inc(S["dve_step"], 1)
                    ve.wait_ge(S["dve_step"], step())
                    ve.tensor_scalar(sums[:, at:at + nh], sums[:, at:at + nh], -SCALE, None, ALU.mult)\
                        .then_inc(S["score_max"], 1)

                def probs(br, part):
                    nb = 2 * l + br
                    ve.wait_ge(S["score_exp"], 6 * nb + 2 * part + 2)
                    at, n = ((0, H2), (H2, 4), (H2 + 4, 4))[part]
                    w = sums[:, 32 + at:32 + at + n]
                    h0 = (0, 0, 4)[part]
                    softmax_scale(l, sums[:, 16 + at:16 + at + n], w, gate_cols(1 + br)[:, min(part, 1), h0:h0 + n])
                    pr = pr1[:, h0:h0 + 4, :] if part else pr0[:, :, :]
                    ve.tensor_tensor(pr, pr, w.unsqueeze(2).to_broadcast([P, n, T if part else P]), ALU.mult)\
                        .then_inc(S["prob_done"], 1)

                def keep_turned(br, n):
                    nb = 2 * l + br
                    ve.wait_ge(S["p_turned"], 6 * nb + n + 1)
                    if n == 1 and br:
                        ve.wait_ge(S["av2_done"], 4 * nb)
                    part, half = TURNS[n]
                    h0 = 4 * half
                    into = (pt0[:, h0:h0 + 4, 0:P], pt0[:, h0:h0 + 4, P:T], pt1[:, h0:h0 + 4, :])[part]
                    ve.tensor_copy(into, bank[3][:, :].rearrange("p (h t) -> p h t", h=4)).then_inc(S["p_kept_v"], 1)

                lo_at(c0 + 34)
                lo_at(c0 + 35)
                score_max(0, 0)
                score_max(0, 1)
                lo_at(c0 + 36)
                score_max(0, 2)
                score_max(0, 3)
                probs(0, 0)
                ve.wait_ge(S["cmp_rot"], l + 1)
                rope(kcmp[0:ROT, :, :], sin_e, cos_e, bank[7][0:ROT, 64:96].rearrange("p (g n) -> p g n", g=2),
                     [ROT, 2, 16]).then_inc(S["cmp_ready"], 1)
                lo_at(c0 + 37)
                score_max(0, 4)
                score_max(0, 5)
                probs(0, 1)
                ve.wait_ge(S["c_score"], l + 1)
                sc = bank[0][:, 0:256].rearrange("p (u n) -> p u n", n=16)
                pc = prc[:, :, :, :].rearrange("p t h n -> p (t h) n")
                c_max, c_sum, c_w = small[:, 0:16], small[:, 16:32], small[:, 48:64]
                ve.tensor_reduce(c_max, sc, AX.X, ALU.max).then_inc(S["dve_step"], 1)
                ve.wait_ge(S["dve_step"], step())
                ve.tensor_scalar(c_max, c_max, -1e20, None, ALU.max).then_inc(S["dve_step"], 1)
                ve.wait_ge(S["dve_step"], step())
                ve.tensor_tensor(pc, sc, c_max.unsqueeze(2).to_broadcast([P, 16, 16]), ALU.subtract)\
                    .then_inc(S["c_diff"], 1)
                probs(0, 2)
                ve.wait_ge(S["c_exp"], l + 1)
                ve.tensor_reduce(c_sum, pc, AX.X, ALU.add).then_inc(S["dve_step"], 1)
                ve.wait_ge(S["dve_step"], step())
                softmax_scale(l, c_sum.rearrange("p (t h) -> p t h", h=H2), c_w.rearrange("p (t h) -> p t h", h=H2),
                              gate_cols(0))
                ve.tensor_tensor(pc, pc, c_w.unsqueeze(2).to_broadcast([P, 16, 16]), ALU.mult).then_inc(S["c_prob"], 1)
                keep_turned(0, 1)
                score_max(1, 0)
                score_max(1, 1)
                keep_turned(0, 3)
                keep_turned(0, 5)
                score_max(1, 2)
                score_max(1, 3)
                for b in range(4):
                    hs2 = slice(2 * b, 2 * b + 2)
                    ve.wait_ge(S["fin_hi_done"], 8 * l + b + 1)
                    ve.tensor_tensor(fin_lo[:, hs2, :], scratch[:, hs2, :], fin_hi[:, hs2, :].bitcast(F32), ALU.subtract)\
                        .then_inc(S["fin_done"], 1)
                probs(1, 0)
                score_max(1, 4)
                score_max(1, 5)
                probs(1, 1)
                keep_turned(1, 1)
                probs(1, 2)
                keep_turned(1, 3)
                keep_turned(1, 5)
                for hp in range(4):
                    hs2 = slice(2 * hp, 2 * hp + 2)
                    ve.wait_ge(S["av2_done"], 8 * l + 4 + hp + 1)
                    ve.tensor_tensor(scratch[:, hs2, :], bank[4 + hp][:, :].rearrange("p (h t) -> p h t", h=2),
                                     snz[:, hs2, :], ALU.mult).then_inc(S["n_gated"], 1)
                for hp in range(4):
                    hs2 = slice(2 * hp, 2 * hp + 2)
                    ve.wait_ge(S["fin_hi_done"], 8 * l + 4 + hp + 1)
                    ve.tensor_tensor(fin_lo[:, H2 + 2 * hp:H2 + 2 * hp + 2, :], scratch[:, hs2, :],
                                     fin_hi[:, H2 + 2 * hp:H2 + 2 * hp + 2, :].bitcast(F32), ALU.subtract)\
                        .then_inc(S["fin_done"], 1)
                for i in range(35, 42):
                    lo_at(c0 + i + 3)
                recip(f"post{l}")
                n = N[f"post{l}"]
                ve.wait_ge(S["recip_done"], n + 1)
                for k in range(KB + 1):
                    if k < KB:
                        ve.scalar_tensor_tensor(scratch[:, k, :], y_out[:, k, :],
                                                col("post")[:, 8 * l + k:8 * l + k + 1], rstd[n % 2][:, :],
                                                ALU.mult, ALU.mult).then_inc(S["scaled"], 1)
                    if k:
                        ve.wait_ge(S["scaled"], 8 * NSC[f"post{l}"] + k)
                        ve.tensor_tensor(x[:, k - 1, :], x[:, k - 1, :], scratch[:, k - 1, :], ALU.add)\
                            .then_inc(S["x_done"], 1)
            for n in (1, 3):
                ve.wait_ge(S["x_out_turned"], n + 1)
                ve.tensor_copy(x_out[:, n // 2, 512:D], bank[4 + n][:, :]).then_inc(S["x_out_kept"], 1)


_INS = ("x", "c", "ctx", "c_ctx", "ada_w", "ada_b", "norm_g", "ffn_w_gate", "ffn_w_up", "ffn_w_down", "ssd_w_in",
        "ssd_conv_w", "ssd_conv_b", "ssd_a_log", "ssd_dt_bias", "ssd_d", "ssd_norm_g", "ssd_w_out", "pool_w", "pool_b",
        "pool_scale", "final_g", "pre_norm_2", "post_norm_2", "w_in_2", "hgrn_lb_logits_2", "hgrn_out_norm_2",
        "cmp_pos_k_2", "cmp_w1_k_2", "cmp_b1_k_2", "cmp_w2_k_2", "cmp_pos_v_2", "cmp_w1_v_2", "cmp_b1_v_2",
        "cmp_w2_v_2", "w_out_2")


def kernel(**inputs):
    import numpy as _np
    import concourse.bacc as _bacc
    from concourse import mybir as _mybir
    from concourse.bass_utils import run_bass_kernel_spmd as _run

    nc = _bacc.Bacc("TRN2", target_bir_lowering=False, num_devices=1)
    arrays = {name: _np.ascontiguousarray(inputs[name]) for name in _INS}
    arrays["shape_consts"], arrays["level_masks"], arrays["pool_tables"] = shape_constants()
    aps = {name: nc.dram_tensor(f"in_{name}", v.shape, _mybir.dt.from_np(v.dtype), kind="ExternalInput").ap()
           for name, v in arrays.items()}
    out = nc.dram_tensor("out_0", (1, T, D), F32, kind="ExternalOutput").ap()
    two_block_kernel(nc, aps, out)
    r = _run(nc, [{f"in_{name}": v for name, v in arrays.items()}], core_ids=[0])
    return r.results[0]["out_0"]
```
